# Optimizing a Trainium2 kernel written in Bass

```python
import functools
import jax, jax.numpy as jnp
from jax import lax
import numpy as np

D_MODEL = 1024
BATCH = 1
SEQ = 1024
DEPTH = 1
DEC_BATCH = 8
DEC_SEQ = 4
PAST_LEN = 2048
PAGE_SIZE = 128

N_HEADS = 16
N_KV_HEADS = 4
HEAD_DIM = D_MODEL // N_HEADS
GQA_GROUP = N_HEADS // N_KV_HEADS
WINDOW = 128
ATTN_W = N_HEADS * HEAD_DIM
KV_W = N_KV_HEADS * HEAD_DIM
D_CONV = D_MODEL
CONV_W = 3
IN_SIZES = (ATTN_W, KV_W, KV_W, D_CONV, D_CONV, D_CONV, ATTN_W, D_CONV)
IN_SPLITS = (ATTN_W, ATTN_W + KV_W, ATTN_W + 2 * KV_W, ATTN_W + 2 * KV_W + D_CONV,
             ATTN_W + 2 * KV_W + 2 * D_CONV, ATTN_W + 2 * KV_W + 3 * D_CONV,
             2 * ATTN_W + 2 * KV_W + 3 * D_CONV)
IN_W = 2 * ATTN_W + 2 * KV_W + 4 * D_CONV
PEER_HEADS = 8
PEER_KEYS = 128
PEER_EXPERTS = PEER_KEYS * PEER_KEYS
PEER_TOPK = 16
PEER_DKEY = 128
PEER_HALF = PEER_DKEY // 2
PEER_BLOCK = 256
RMS_EPS = 1e-6

kernel_name = "hybrid_swa_shortconv_peer_adaln_step"

def rms_norm(x, w):
    xf = x.astype(jnp.float32)
    y = xf * lax.rsqrt(jnp.mean(xf * xf, axis=-1, keepdims=True) + RMS_EPS)
    return (y * w.astype(jnp.float32)).astype(x.dtype)

def adaln(c, w_ada, b_ada):
    mod = jax.nn.silu(c) @ w_ada + b_ada
    return jnp.split(mod[:, None, :], 6, axis=-1)

def sink_attention(q, k, v, mask, sinks):
    s = jnp.einsum('...qhgd,...khd->...hgqk', q, k).astype(jnp.float32) * (HEAD_DIM ** -0.5)
    s = jnp.where(mask[..., None, None, :, :], s, -jnp.inf)
    sink = sinks.astype(jnp.float32).reshape(N_KV_HEADS, GQA_GROUP, 1, 1)
    m = jnp.maximum(jnp.max(s, axis=-1, keepdims=True), sink)
    p = jnp.exp(s - m)
    denom = jnp.sum(p, axis=-1, keepdims=True) + jnp.exp(sink - m)
    o = jnp.einsum('...hgqk,...khd->...qhgd', p / denom, v.astype(jnp.float32))
    return o.astype(q.dtype)

def prompt_attend(q, k, v, sinks):
    b, s = q.shape[:2]
    nb = s // WINDOW
    qb = q.reshape(b, nb, WINDOW, N_KV_HEADS, GQA_GROUP, HEAD_DIM)
    kb = k.reshape(b, nb, WINDOW, N_KV_HEADS, HEAD_DIM)
    vb = v.reshape(b, nb, WINDOW, N_KV_HEADS, HEAD_DIM)
    pad = ((0, 0), (1, 0), (0, 0), (0, 0), (0, 0))
    kk = jnp.concatenate([jnp.pad(kb, pad)[:, :-1], kb], axis=2)
    vv = jnp.concatenate([jnp.pad(vb, pad)[:, :-1], vb], axis=2)
    qi = jnp.arange(WINDOW)[:, None] + WINDOW
    kj = jnp.arange(2 * WINDOW)[None, :]
    rel = qi - kj
    band = (rel >= 0) & (rel < WINDOW)
    valid = (jnp.arange(nb)[:, None, None] * WINDOW + kj[None] - WINDOW) >= 0
    mask = band[None] & valid
    o = sink_attention(qb, kk, vv, mask, sinks)
    return o.reshape(b, s, ATTN_W), k[:, -WINDOW:], v[:, -WINDOW:]

def sample_attend(q, k, v, sinks, cache_k, cache_v):
    db, L = q.shape[:2]
    kk = jnp.concatenate([cache_k.astype(k.dtype), k], axis=1)
    vv = jnp.concatenate([cache_v.astype(v.dtype), v], axis=1)
    rel = (jnp.arange(L)[:, None] + WINDOW) - jnp.arange(WINDOW + L)[None, :]
    mask = (rel >= 0) & (rel < WINDOW)
    o = sink_attention(q.reshape(db, L, N_KV_HEADS, GQA_GROUP, HEAD_DIM), kk, vv, mask, sinks)
    return o.reshape(db, L, ATTN_W), kk[:, -WINDOW:], vv[:, -WINDOW:]

def short_conv(u, prev, w, bias):
    L = u.shape[1]
    up = jnp.concatenate([prev.astype(u.dtype), u], axis=1)
    y = up[:, 0:L] * w[0] + up[:, 1:L + 1] * w[1] + up[:, 2:L + 2] * w[2] + bias
    return y, up[:, -(CONV_W - 1):]

def peer_ffn(h, w_query, sub_keys, expert_u, expert_v):
    shp = h.shape
    t = h.reshape(-1, D_MODEL)
    n = t.shape[0]
    t = jnp.pad(t, ((0, (-n) % PEER_BLOCK), (0, 0)))
    blocks = t.reshape(-1, PEER_BLOCK, D_MODEL)
    keys = sub_keys.astype(jnp.float32)

    def one_block(xb):
        q = (xb @ w_query).reshape(PEER_BLOCK, PEER_HEADS, 2, PEER_HALF).astype(jnp.float32)
        s = jnp.einsum('thcd,hcnd->thcn', q, keys)
        sv, si = lax.top_k(s, PEER_TOPK)
        cand = sv[:, :, 0, :, None] + sv[:, :, 1, None, :]
        cv, ci = lax.top_k(cand.reshape(PEER_BLOCK, PEER_HEADS, PEER_TOPK * PEER_TOPK), PEER_TOPK)
        i1 = jnp.take_along_axis(si[:, :, 0], ci // PEER_TOPK, axis=-1)
        i2 = jnp.take_along_axis(si[:, :, 1], ci % PEER_TOPK, axis=-1)
        idx = i1 * PEER_KEYS + i2
        g = jax.nn.softmax(cv, axis=-1)
        a = jax.nn.gelu(jnp.einsum('thkd,td->thk', expert_u[idx], xb).astype(jnp.float32), approximate=False)
        wgt = (g * a).astype(xb.dtype)
        return jnp.einsum('thk,thkd->td', wgt, expert_v[idx])

    out = lax.map(one_block, blocks)
    return out.reshape(-1, D_MODEL)[:n].reshape(shp)

def block(x, c, conv_prev, attend, w_ada, b_ada, norm1_w, w_in, q_norm_w, k_norm_w, sinks,
          conv_w, conv_bias, w_out, norm2_w, w_query, sub_keys, expert_u, expert_v):
    b, L, _ = x.shape
    sh1, sc1, g1, sh2, sc2, g2 = adaln(c, w_ada, b_ada)
    h = rms_norm(x, norm1_w) * (1 + sc1) + sh1
    z = h @ w_in
    q, k, v, u, gate_post, gate_pre, g_attn, g_conv = jnp.split(z, IN_SPLITS, axis=-1)
    q = rms_norm(q.reshape(b, L, N_HEADS, HEAD_DIM), q_norm_w)
    k = rms_norm(k.reshape(b, L, N_KV_HEADS, HEAD_DIM), k_norm_w)
    v = v.reshape(b, L, N_KV_HEADS, HEAD_DIM)
    o_attn, new_k, new_v = attend(q, k, v, sinks)
    conv_y, new_conv = short_conv(gate_pre * u, conv_prev, conv_w, conv_bias)
    o_conv = gate_post * conv_y
    merged = jax.nn.sigmoid(g_attn) * o_attn + jax.nn.sigmoid(g_conv) * o_conv
    x = x + g1 * (merged @ w_out)
    h2 = rms_norm(x, norm2_w) * (1 + sc2) + sh2
    x = x + g2 * peer_ffn(h2, w_query, sub_keys, expert_u, expert_v)
    return x, new_k, new_v, new_conv

def setup_inputs(seed: int = 0) -> dict:
    key = jax.random.key(seed)
    ks = jax.random.split(key, 24)
    nrm = lambda k, shape, scale: jax.random.normal(k, shape, jnp.float32) * scale
    return {
        'x_prompt': nrm(ks[0], (BATCH, SEQ, D_MODEL), 1.0),
        'x_sample': nrm(ks[1], (DEC_BATCH, DEC_SEQ, D_MODEL), 1.0),
        'cache_k': nrm(ks[2], (DEPTH, DEC_BATCH, WINDOW, N_KV_HEADS, HEAD_DIM), 1.0),
        'cache_v': nrm(ks[3], (DEPTH, DEC_BATCH, WINDOW, N_KV_HEADS, HEAD_DIM), 1.0),
        'state_conv': nrm(ks[4], (DEPTH, DEC_BATCH, CONV_W - 1, D_CONV), 1.0),
        'c_prompt': nrm(ks[5], (BATCH, D_MODEL), 1.0),
        'c_sample': nrm(ks[6], (DEC_BATCH, D_MODEL), 1.0),
        'w_ada': nrm(ks[7], (DEPTH, D_MODEL, 6 * D_MODEL), D_MODEL ** -0.5),
        'b_ada': nrm(ks[8], (DEPTH, 6 * D_MODEL), 0.02),
        'norm1_w': 1.0 + nrm(ks[9], (DEPTH, D_MODEL), 0.02),
        'w_in': nrm(ks[10], (DEPTH, D_MODEL, IN_W), D_MODEL ** -0.5),
        'q_norm_w': 1.0 + nrm(ks[11], (DEPTH, HEAD_DIM), 0.02),
        'k_norm_w': 1.0 + nrm(ks[12], (DEPTH, HEAD_DIM), 0.02),
        'sinks': nrm(ks[13], (DEPTH, N_HEADS), 1.0),
        'conv_w': nrm(ks[14], (DEPTH, CONV_W, D_CONV), CONV_W ** -0.5),
        'conv_bias': nrm(ks[15], (DEPTH, D_CONV), 0.02),
        'w_out': nrm(ks[16], (DEPTH, ATTN_W, D_MODEL), ATTN_W ** -0.5),
        'norm2_w': 1.0 + nrm(ks[17], (DEPTH, D_MODEL), 0.02),
        'w_query': nrm(ks[18], (DEPTH, D_MODEL, PEER_HEADS * PEER_DKEY), D_MODEL ** -0.5),
        'sub_keys': nrm(ks[19], (DEPTH, PEER_HEADS, 2, PEER_KEYS, PEER_HALF), PEER_HALF ** -0.5),
        'expert_u': nrm(ks[20], (DEPTH, PEER_EXPERTS, D_MODEL), D_MODEL ** -0.5),
        'expert_v': nrm(ks[21], (DEPTH, PEER_EXPERTS, D_MODEL), 1.0),
    }

def reference(x_prompt, x_sample, cache_k, cache_v, state_conv, c_prompt, c_sample,
              w_ada, b_ada, norm1_w, w_in, q_norm_w, k_norm_w, sinks, conv_w, conv_bias,
              w_out, norm2_w, w_query, sub_keys, expert_u, expert_v):
    yp, ys = x_prompt, x_sample
    kp, vp, cp, ksm, vsm, csm = [], [], [], [], [], []
    for l in range(DEPTH):
        lw = (w_ada[l], b_ada[l], norm1_w[l], w_in[l], q_norm_w[l], k_norm_w[l], sinks[l],
              conv_w[l], conv_bias[l], w_out[l], norm2_w[l], w_query[l], sub_keys[l],
              expert_u[l], expert_v[l])
        conv0 = jnp.zeros((yp.shape[0], CONV_W - 1, D_CONV), yp.dtype)
        yp, k1, v1, c1 = block(yp, c_prompt, conv0, prompt_attend, *lw)
        attend_s = functools.partial(sample_attend, cache_k=cache_k[l], cache_v=cache_v[l])
        ys, k2, v2, c2 = block(ys, c_sample, state_conv[l], attend_s, *lw)
        kp.append(k1); vp.append(v1); cp.append(c1)
        ksm.append(k2); vsm.append(v2); csm.append(c2)
    return (yp, ys, jnp.stack(kp), jnp.stack(vp), jnp.stack(cp), jnp.stack(ksm), jnp.stack(vsm), jnp.stack(csm))


_drawn_inputs = setup_inputs


def setup_inputs(seed=0):
    import zlib

    import numpy as np

    out = dict(_drawn_inputs(seed))
    spreads = {}
    factors = {'q_norm_w': 6.742, 'k_norm_w': 3.052, 'sinks': 28.53}
    for name, (base, spread) in spreads.items():
        noise = np.random.default_rng([zlib.crc32(name.encode()), seed]).standard_normal(out[name].shape)
        drawn = base * np.exp(spread * noise) if base else spread * noise
        out[name] = __import__('jax').numpy.asarray(drawn.astype(out[name].dtype))
    for name, factor in factors.items():
        out[name] = (out[name] * factor).astype(out[name].dtype)
    return out
```

```python
from contextlib import ExitStack

import concourse.bass as bass
from concourse import mybir

F32 = mybir.dt.float32
I32 = mybir.dt.int32
U32 = mybir.dt.uint32
ALU = mybir.AluOpType
ACT = mybir.ActivationFunctionType
AX = mybir.AxisListType

P = 128
D = 1024
KC = D // P
NP = 1024
NT = NP // P
NB, L = 8, 4
NS = NB * L
T = NP + NS
NH, NKV, HD = 16, 4, 64
KVW = NKV * HD
QKV = D + 2 * KVW
NQK = NH + NKV
WIN = 128
EPS = 1e-6
SCALE = HD ** -0.5
NEG = -1e30
LOWEST = -3.0e38
PH, PK, TOPK = 8, 128, 16
NE = PK * PK
RING = 8
ABLK = 512
NBLK = 6 * D // ABLK
ARING = 3
ENGINES = 5
ARENA = 33500


def build(nc, x_prompt, x_sample, cache_k, cache_v, state_conv, c_prompt, c_sample,
          w_ada, b_ada, norm1_w, w_in, q_norm_w, k_norm_w, sinks, conv_w, conv_bias,
          w_out, norm2_w, w_query, sub_keys, expert_u, expert_v,
          y_prompt, y_sample, new_k_prompt, new_v_prompt, new_conv_prompt,
          new_k_sample, new_v_sample, new_conv_sample):
    xp = x_prompt.rearrange("a (t p) d -> (a t) p d", p=P)
    xs = x_sample.rearrange("b l d -> (b l) d")
    yp = y_prompt.rearrange("a (t p) d -> (a t) p d", p=P)
    ys = y_sample.rearrange("b l d -> (b l) d")
    ck = cache_k.rearrange("a b w g d -> (a b) w (g d)")
    cv = cache_v.rearrange("a b w g d -> (a b) w (g d)")
    nks = new_k_sample.rearrange("a b w g d -> (a b) w (g d)")
    nvs = new_v_sample.rearrange("a b w g d -> (a b) w (g d)")
    w_ada_v = w_ada.rearrange("a (k p) n -> (a p) k n", p=P)
    w_in_v = w_in.rearrange("a (k p) n -> (a p) k n", p=P)
    w_out_v = w_out.rearrange("a (k p) n -> (a p) k n", p=P)
    w_query_v = w_query.rearrange("a (k p) n -> (a p) k n", p=P)
    keys_v = sub_keys.rearrange("a h c n d -> (a h) c n d")
    eu = expert_u.rearrange("a n d -> (a n) d")
    ev = expert_v.rearrange("a n d -> (a n) d")

    mod_p = nc.dram_tensor("mod_p", [1, 6 * D], F32, kind="Internal").ap()
    mod_s = nc.dram_tensor("mod_s", [NS, 6 * D], F32, kind="Internal").ap()
    x2_d = nc.dram_tensor("x2_d", [NT + 1, P, D], F32, kind="Internal").ap()
    h2_d = nc.dram_tensor("h2_d", [NT + 1, P, D], F32, kind="Internal").ap()

    ctx = ExitStack()
    with ctx:
        def sb(name, shape, dt=F32):
            return ctx.enter_context(nc.sbuf_tensor(name, shape, dt))

        def sem(name):
            return ctx.enter_context(nc.semaphore(name))

        ident = sb("ident", [P, P])
        sel_s = sb("sel_s", [P, NS])
        eps = sb("eps", [P, 1])
        tokens_t = sb("tokens_t", [P, KC * (NT + 1) * P])
        hT = tokens_t[:, 0:KC * T].rearrange("p (k t) -> p k t", k=KC)
        query_t = tokens_t[:, :]
        oT = sb("oT", [P, KC, T])
        state_t = sb("state_t", [P, KC, NB * 2])
        new_t = sb("new_t", [P, KC, 2 + NB * 2])
        cw = sb("cw", [P, 4, KC])
        arena = sb("arena", [P, ARENA])
        cursor = [0]

        def carve(*shape):
            n = 1
            for s in shape:
                n *= s
            v = arena[:, cursor[0]:cursor[0] + n]
            cursor[0] += n
            assert cursor[0] <= ARENA, cursor[0]
            if len(shape) == 2:
                v = v.rearrange("p (a b) -> p a b", a=shape[0])
            if len(shape) == 3:
                v = v.rearrange("p (a b c) -> p a b c", a=shape[0], b=shape[1])
            if len(shape) == 4:
                v = v.rearrange("p (a b c d) -> p a b c d", a=shape[0], b=shape[1], c=shape[2])
            return v

        bank = ctx.enter_context(nc.psum_tensor("bank", [P, 8, 512], F32))

        def banks(a, n):
            return bank[:, a:a + n, :].rearrange("p a b -> p (a b)")

        passed = {e: sem(f"passed_{e}") for e in ("sp", "act", "dve", "pe", "pool")}
        stage_end = [sem(f"stage_end_{s}") for s in "ABSCD"]
        chain_dve, chain_act, chain_pool = sem("chain_dve"), sem("chain_act"), sem("chain_pool")

        def hold(eng, who, s, value):
            eng.wait_ge(s, value)
            eng.sem_inc(passed[who], 1)

        class Chain:
            def __init__(self, eng, s):
                self.eng, self.s, self.n = eng, s, 0

            def __call__(self, ins):
                self.n += 1
                ins.then_inc(self.s, 1)
                self.eng.wait_ge(self.s, self.n)

            def note(self, ins):
                self.n += 1
                ins.then_inc(self.s, 1)

            def settle(self):
                if self.n:
                    self.eng.wait_ge(self.s, self.n)

            def restart(self):
                self.settle()
                self.eng.sem_clear(self.s)
                self.n = 0

        def barrier(eng, s):
            eng.drain().then_inc(stage_end[s], 1)
            eng.wait_ge(stage_end[s], ENGINES)

        def scr(region, at, *shape):
            n = 1
            for s in shape:
                n *= s
            v = region[:, at:at + n]
            if len(shape) == 2:
                v = v.rearrange("p (a b) -> p a b", a=shape[0])
            return v, at + n

        w_qkv = carve(KC, QKV)
        mark_qkv = cursor[0]
        ada_w = [carve(KC, ABLK) for _ in range(ARING)]
        mod9 = carve(6 * D)
        bada9 = tokens_t[:, 0:6 * D]
        o_flat = oT[:, :, :].rearrange("p k t -> p (k t)")
        c9, at = scr(o_flat, 0, D)
        ec9, at = scr(o_flat, at, D)
        st16, at = scr(o_flat, at, D)
        cw4, at = scr(o_flat, at, D)
        cT, at = scr(o_flat, at, KC, NB + 1)

        cursor[0] = mark_qkv
        xt = [carve(D) for _ in range(2)]
        h_row = carve(D)
        A1 = [carve(D) for _ in range(2)]
        B1 = [carve(D) for _ in range(2)]
        qkv = carve(QKV)
        sq = carve(NQK, HD)
        junk = sq[:, :, :].rearrange("p h d -> p (h d)")[:, 0:D]
        qk_w = carve(NQK, HD)
        smax, nmax, sdif, esink, den, rden = (carve(4) for _ in range(6))
        ssq, rms, rstd = carve(1), carve(1), carve(1)
        hss, hrms, hrs = carve(NQK), carve(NQK), carve(NQK)
        mark_attn = cursor[0]
        hT_now = carve(KC, P)
        kpad = carve(NKV, 2, 2, P)
        vpad = carve(2, NKV, 3 * HD)
        maskt = carve(3, 2, P)
        sink_row = carve(NH)
        qT_now = carve(KC, P)
        sm, pe_ = carve(4, 2 * P), carve(4, 2 * P)
        pT = carve(2, 4, P)
        cursor[0] = mark_attn
        ck_sb, cv_sb = carve(NB, KVW), carve(NB, KVW)
        kcT = carve(NKV, NB * WIN + NS)
        s_mask = carve(NB * WIN + NS)
        qz = xt[1][:, 0:NKV * P].rearrange("p (g r e t) -> p g r e t", g=NKV, r=2, e=2)
        sink_col = carve(NKV)
        cursor[0] = 0
        s_sm, s_pT = carve(NB * WIN + NS), carve(NB + 1, P)
        cursor[0] = 0
        w_c = [carve(KC, P) for _ in range(5)]
        u_sb, y_c, sg_c, sg_a, mg = (carve(T) for _ in range(5))
        cu_p = carve(2 + NP)
        cu_s = carve(NB, 2 + L)
        cw_now = carve(4)
        cursor[0] = max(cursor[0], mark_qkv)
        wo_sb, wq_sb = carve(KC, D), carve(KC, D)
        cursor[0] = 0
        mT = carve(KC, P)
        xd = [carve(D) for _ in range(2)]
        G1, A2, B2, n2 = carve(D), carve(D), carve(D), carve(D)
        x2, h2, h2T, junk2 = carve(D), carve(D), carve(KC, P), carve(D)
        ssq2, rms2, rstd2 = carve(1), carve(1), carve(1)
        assert cursor[0] <= mark_qkv
        cursor[0] = 0
        u_ring = [carve(D) for _ in range(RING)]
        v_ring = [carve(D) for _ in range(RING)]
        h2_next, h2_now, x2_now, y_now, prod = carve(D), carve(D), carve(D), carve(D), carve(2, D)
        G2 = carve(D)
        diag = [carve(P) for _ in range(RING)]
        keys_bd = carve(PH + 1, 2 * PK)
        keys_row = u_ring[0][:, :].rearrange("p (h c) -> p h c", h=PH)
        q_st = [carve(P) for _ in range(2)]
        s_sb = [carve(2, PK) for _ in range(2)]
        s_cut, cand, cand_cut, onehot = carve(PK), carve(TOPK, TOPK), carve(TOPK, TOPK), carve(TOPK, TOPK)
        top_v, top_f = carve(2, TOPK), carve(2, TOPK)
        top_i = carve(2, TOPK).bitcast(U32)
        best_v, best_f = carve(TOPK), carve(TOPK)
        best_i, part_i = carve(TOPK).bitcast(U32), carve(TOPK).bitcast(U32)
        i_half = carve(2, TOPK)
        iota16 = carve(TOPK)
        idx = [carve(TOPK).bitcast(I32) for _ in range(2)]
        idx_s = [carve(4).bitcast(I32) for _ in range(2)]
        gate, gate_e, gsum, nbest = carve(TOPK), carve(TOPK), carve(1), carve(1)
        gate_s = carve(4)
        dot, act_dot, wgt = carve(TOPK), carve(TOPK), carve(TOPK)
        zeros_bf = carve(P // 2).bitcast(mybir.dt.bfloat16)
        zmov_bf = carve(256).bitcast(mybir.dt.bfloat16)

        consts_made, small_in, qkv_w_in, keys_in = sem("consts_made"), sem("small_in"), sem("qkv_w_in"), sem("keys_in")
        ada_in = [sem(f"ada_in_{r}") for r in range(ARING)]
        exp_c, silu_made, small_ps, small_made = sem("exp_c"), sem("silu_made"), sem("small_in_psum"), sem("small_made")
        ada_free, ada_ps, mod_stored = sem("ada_free"), sem("ada_in_psum"), sem("mod_stored")
        rows_in, scale1_made, attn_zeroed = sem("rows_in"), sem("scale1_made"), sem("attn_zeroed")
        x_in = [sem(f"x_in_{u}") for u in range(2)]
        x_free, rms_made, h_made, hT_ps, hT_copied, hT_kept = (sem(n) for n in (
            "x_free", "rms_made", "h_made", "hT_in_psum", "hT_copied", "hT_kept"))
        qkv_ps, qkv_out, qkv_free, hss_made, hrms_made, qk_normed, v_placed = (sem(n) for n in (
            "qkv_in_psum", "qkv_out", "qkv_free", "head_sums", "head_rms", "qk_normed", "v_placed"))
        qkT_ps, qT_made, kpad_made, score_ps, score_read, max_made, exp_made, den_made, p_made = (sem(n) for n in (
            "qkT_in_psum", "qT_made", "kpad_made", "scores_in_psum", "scores_read", "max_made", "exp_made",
            "den_made", "p_made"))
        pT_ps, pT0_made, pT1_made, pv_ps, o_kept, kv_stored = (sem(n) for n in (
            "pT_in_psum", "pT0_made", "pT1_made", "pv_in_psum", "o_kept", "kv_stored"))
        sx_in, scache_in, s_rows, s_act, s_dve, s_pe, s_stored = (sem(n) for n in (
            "s_x_in", "s_cache_in", "s_rows", "s_act_step", "s_dve_step", "s_pe_step", "s_stored"))
        s_kc0, s_kc1, s_kcps, mask_s_made = sem("s_kc0"), sem("s_kc1"), sem("s_kc_in_psum"), sem("mask_s_made")
        wc_in = [sem(f"wc_in_{r}") for r in range(5)]
        wc_free, conv_ps, conv_read, u_made, gate_c_made, gate_a_made, cu_made = (sem(n) for n in (
            "wc_free", "conv_in_psum", "conv_read", "u_made", "gate_c_made", "gate_a_made", "cu_made"))
        d_w_in, d_rows, new_ps, new_made, new_stored = (sem(n) for n in (
            "d_weights_in", "d_rows_in", "new_conv_in_psum", "new_conv_made", "new_conv_stored"))
        xd_in = [sem(f"xd_in_{u}") for u in range(2)]
        mT_made, xd_free, out_ps, x2_made, rms2_made, h2_made, h2T_ps, h2T_made, qry_ps, qry_kept, rows_made = (
            sem(n) for n in ("mT_made", "xd_free", "out_in_psum", "x2_made", "rms2_made", "h2_made",
                             "h2T_in_psum", "h2T_made", "query_in_psum", "query_kept", "d_rows_made"))
        x2h2_stored = sem("x2h2_stored")
        e_consts, e_keys_ps, e_keys_made, e_g2_in = (sem(n) for n in (
            "e_consts", "keys_in_psum", "keys_made", "g2_in"))
        u_in = [sem(f"u_in_{r}") for r in range(RING)]
        v_in = [sem(f"v_in_{r}") for r in range(RING)]
        u_free, v_free, q_staged, s_ps, s_out, best_made, gate_exp, idx_made, gelu_made, wgt_made, diag_made = (
            sem(n) for n in ("u_free", "v_free", "q_staged", "s_in_psum", "s_out", "best_made", "gate_exp",
                             "idx_made", "gelu_made", "wgt_made", "diag_made"))
        y_ps, y_read, y_made, y_stored, y_free, h2_in, h2_taken, x2_in, idx_s_made = (sem(n) for n in (
            "y_in_psum", "y_read", "y_made", "y_stored", "y_free", "h2_in", "h2_taken", "x2_in", "idx_s_made"))

        block = ctx.enter_context(nc.Block())

        C_U, C_POST, C_PRE, C_GA, C_GC = QKV, QKV + D, QKV + 2 * D, QKV + 3 * D, QKV + 4 * D
        C_KINDS = [C_U, C_PRE, C_POST, C_GC, C_GA]

        @block.sync
        def _(sp):
            sp.dma_start(c9[0:NB, :], c_sample).then_inc(small_in, 16)
            sp.dma_start(c9[NB:NB + 1, :], c_prompt).then_inc(small_in, 16)
            sp.dma_start(st16[0:NB * 2, :], state_conv.rearrange("a b r d -> (a b r) d")).then_inc(small_in, 16)
            sp.dma_start(cw4[0:3, :], conv_w.rearrange("a r d -> (a r) d")).then_inc(small_in, 16)
            sp.dma_start(cw4[3:4, :], conv_bias).then_inc(small_in, 16)
            sp.dma_start(bada9[0:NB + 1, :], b_ada.to_broadcast([NB + 1, 6 * D])).then_inc(small_in, 16)
            with sp.Fori(0, NBLK // ARING) as j:
                for r in range(ARING):
                    hold(sp, "sp", ada_free, j * ARING + r + 1)
                    sp.dma_start(ada_w[r][:, :, :], w_ada_v[:, :, bass.ds(j * (ARING * ABLK) + r * ABLK, ABLK)]
                                 ).then_inc(ada_in[r], 16)
            sp.dma_start(w_qkv[:, :, :], w_in_v[:, :, 0:QKV]).then_inc(qkv_w_in, 16)
            barrier(sp, 0)
            sp.dma_start(A1[0][:, :], mod_p[:, D:2 * D].to_broadcast([P, D])).then_inc(rows_in, 16)
            sp.dma_start(B1[0][:, :], mod_p[:, 0:D].to_broadcast([P, D])).then_inc(rows_in, 16)
            sp.dma_start(A1[1][0:NS, :], mod_s[:, D:2 * D]).then_inc(rows_in, 16)
            sp.dma_start(B1[1][0:NS, :], mod_s[:, 0:D]).then_inc(rows_in, 16)
            sp.dma_start(junk[:, :], norm1_w.to_broadcast([P, D])).then_inc(rows_in, 16)
            sp.dma_start(qk_w[:, 0, :], q_norm_w.to_broadcast([P, HD])).then_inc(rows_in, 16)
            sp.dma_start(qk_w[:, NH, :], k_norm_w.to_broadcast([P, HD])).then_inc(rows_in, 16)
            sp.dma_start(sink_row[:, :], sinks.to_broadcast([P, NH])).then_inc(rows_in, 16)
            with sp.Fori(0, NT // 2) as i:
                for u in range(2):
                    hold(sp, "sp", x_free, i * 2 + u + 1)
                    sp.dma_start(xt[u][:, :], xp[bass.ds(i * 2 + u, 1), :, :].rearrange("a p d -> (a p) d")
                                 ).then_inc(x_in[u], 16)
            sp.wait_ge(qk_normed, NT)
            sp.dma_start(new_k_prompt.rearrange("a b w g d -> (a b w) (g d)"), qkv[:, D:D + KVW]).then_inc(kv_stored, 16)
            sp.dma_start(new_v_prompt.rearrange("a b w g d -> (a b w) (g d)"), qkv[:, D + KVW:QKV]).then_inc(kv_stored, 16)
            sp.wait_ge(kv_stored, 32)
            barrier(sp, 1)
            sp.dma_start(xt[0][0:NS, :], xs).then_inc(sx_in, 16)
            sp.dma_start(ck_sb[:, :, :], ck.rearrange("b w c -> w b c")).then_inc(scache_in, 16)
            sp.dma_start(cv_sb[:, :, :], cv.rearrange("b w c -> w b c")).then_inc(scache_in, 16)
            with nc.allow_non_contiguous_dma(reason="one sink for each quadrant of rows and group"):
                for q in range(4):
                    sp.dma_start(sink_col[32 * q:32 * q + 32, :],
                                 sinks.rearrange("a (g q) -> a g q", q=4)[:, :, q].to_broadcast([32, NKV])).then_inc(s_rows, 16)
            sp.dma_start(nks[:, 0:WIN - L, :], ck[:, L:WIN, :]).then_inc(s_stored, 16)
            sp.dma_start(nvs[:, 0:WIN - L, :], cv[:, L:WIN, :]).then_inc(s_stored, 16)
            sp.wait_ge(s_dve, 3)
            for b in range(NB):
                sp.dma_start(nks[b, WIN - L:WIN, :], qkv[L * b:L * b + L, D:D + KVW]).then_inc(s_stored, 16)
                sp.dma_start(nvs[b, WIN - L:WIN, :], qkv[L * b:L * b + L, D + KVW:QKV]).then_inc(s_stored, 16)
            sp.wait_ge(s_stored, 16 * (2 + 2 * NB))
            barrier(sp, 2)
            with sp.Fori(0, KC // 2) as i:
                for n in range(10):
                    hold(sp, "sp", wc_free, i * 10 + n + 1)
                    sp.dma_start(w_c[n % 5][:, :, :],
                                 w_in_v[:, :, bass.ds(i * (2 * P) + (C_KINDS[n % 5] + (n // 5) * P), P)]
                                 ).then_inc(wc_in[n % 5], 16)
            sp.dma_start(wo_sb[:, :, :], w_out_v).then_inc(d_w_in, 16)
            sp.dma_start(wq_sb[:, :, :], w_query_v).then_inc(d_w_in, 16)
            barrier(sp, 3)
            sp.dma_start(G1[:, :], mod_p[:, 2 * D:3 * D].to_broadcast([P, D])).then_inc(d_rows, 16)
            sp.dma_start(A2[:, :], mod_p[:, 4 * D:5 * D].to_broadcast([P, D])).then_inc(d_rows, 16)
            sp.dma_start(B2[:, :], mod_p[:, 3 * D:4 * D].to_broadcast([P, D])).then_inc(d_rows, 16)
            sp.dma_start(n2[:, :], norm2_w.to_broadcast([P, D])).then_inc(d_rows, 16)
            with sp.Fori(0, NT // 2) as i:
                for u in range(2):
                    hold(sp, "sp", xd_free, i * 2 + u + 1)
                    sp.dma_start(xd[u][:, :], xp[bass.ds(i * 2 + u, 1), :, :].rearrange("a p d -> (a p) d")
                                 ).then_inc(xd_in[u], 16)
            sp.wait_ge(xd_free, NT + 1)
            sp.dma_start(xd[0][0:NS, :], xs).then_inc(xd_in[0], 16)
            sp.wait_ge(h2_made, NT)
            sp.wait_ge(x2_made, NT)
            sp.dma_start(G1[0:NS, :], mod_s[:, 2 * D:3 * D]).then_inc(d_rows, 16)
            sp.dma_start(A2[0:NS, :], mod_s[:, 4 * D:5 * D]).then_inc(d_rows, 16)
            sp.dma_start(B2[0:NS, :], mod_s[:, 3 * D:4 * D]).then_inc(d_rows, 16)
            barrier(sp, 4)
            sp.dma_start(keys_row[:, :, 0:HD], keys_v[:, 0, :, :].rearrange("h n d -> n h d")).then_inc(keys_in, 16)
            sp.dma_start(keys_row[:, :, HD:P], keys_v[:, 1, :, :].rearrange("h n d -> n h d")).then_inc(keys_in, 16)
            sp.dma_start(G2[:, :], mod_p[:, 5 * D:6 * D].to_broadcast([P, D])).then_inc(e_g2_in, 16)
            sp.dma_start(h2_next[:, :], h2_d[0, :, :]).then_inc(h2_in, 16)
            sp.dma_start(x2_now[:, :], x2_d[0, :, :]).then_inc(x2_in, 16)
            sp.sem_inc(y_free, 1)
            with sp.Fori(0, NT - 1) as t:
                hold(sp, "sp", h2_taken, t + 1)
                sp.dma_start(h2_next[:, :], h2_d[bass.ds(t + 1, 1), :, :].rearrange("a p d -> (a p) d")).then_inc(h2_in, 16)
                hold(sp, "sp", y_made, t + 1)
                sp.dma_start(yp[bass.ds(t, 1), :, :].rearrange("a p d -> (a p) d"), y_now[:, :]).then_inc(y_stored, 16)
                sp.dma_start(x2_now[:, :], x2_d[bass.ds(t + 1, 1), :, :].rearrange("a p d -> (a p) d")).then_inc(x2_in, 16)
                hold(sp, "sp", y_stored, t * 16 + 16)
                sp.sem_inc(y_free, 1)
            sp.wait_ge(h2_taken, NT)
            for q in range(4):
                sp.dma_start(h2_next[NS * q:NS * q + NS, :], h2_d[NT, 0:NS, :]).then_inc(h2_in, 16)
            sp.wait_ge(y_made, NT)
            sp.dma_start(yp[NT - 1, :, :], y_now[:, :]).then_inc(y_stored, 16)
            sp.dma_start(x2_now[0:NS, :], x2_d[NT, 0:NS, :]).then_inc(x2_in, 16)
            sp.dma_start(G2[0:NS, :], mod_s[:, 5 * D:6 * D]).then_inc(e_g2_in, 16)
            sp.wait_ge(y_stored, 16 * NT)
            sp.sem_inc(y_free, 1)
            sp.wait_ge(y_made, NT + 1)
            sp.dma_start(ys, y_now[0:NS, :]).then_inc(y_stored, 16)
            sp.wait_ge(y_stored, 16 * (NT + 1))

        @block.gpsimd
        def _(pool):
            link = Chain(pool, chain_pool)

            def where(view, pattern, base, mult, cmp, fill):
                link(pool.affine_select(out=view, in_=view, compare_op=cmp, fill=fill, base=base,
                                        pattern=pattern, channel_multiplier=mult))

            link(pool.memset(ident[:, :], 0.0))
            where(ident[:, :], [[-1, P]], 0, 1, ALU.not_equal, 1.0)
            link(pool.memset(sel_s[:, :], 0.0))
            for q in range(4):
                where(sel_s[:, :], [[-1, NS]], -NS * q, 1, ALU.not_equal, 1.0)
            link(pool.memset(eps[:, :], EPS))
            pool.sem_inc(consts_made, 1)
            barrier(pool, 0)
            link(pool.memset(maskt[:, :, :, :], 0.0))
            for m, own in ((0, 0), (1, 1), (2, 0)):
                where(maskt[:, m, own, :], [[-1, P]], 0, 1, ALU.is_ge, NEG)
                if m:
                    where(maskt[:, m, 1 - own, :], [[1, P]], -1, -1, ALU.is_ge, NEG)
            link(pool.memset(maskt[:, 0, 1, :], NEG))
            link(pool.memset(kpad[:, :, :, :, :], 0.0))
            link(pool.memset(vpad[:, :, :, :], 0.0))
            pool.sem_inc(attn_zeroed, 1)
            link.restart()
            with pool.Fori(0, NT // 2) as i:
                for u in range(2):
                    t = i * 2 + u
                    hold(pool, "pool", hT_copied, t + 1)
                    link(pool.tensor_copy(hT[:, :, bass.ds(t * P, P)], hT_now[:, :, :]))
                    pool.sem_inc(hT_kept, 1)
                    hold(pool, "pool", qkv_out, t + 1)
                    hold(pool, "pool", pv_ps, t * 4 + 4)
                    for half in range(2):
                        link(pool.tensor_copy(vpad[:, u, :, 2 * HD * half:2 * HD * half + HD],
                                              qkv[:, D + KVW:QKV].rearrange("p (g d) -> p g d", g=NKV)))
                    pool.sem_inc(v_placed, 1)
                link.restart()
            barrier(pool, 1)
            link(pool.memset(s_mask[:, :], 0.0))
            link(pool.memset(qz[:, :, :, :, :], 0.0))
            cache = s_mask[0:NS, 0:NB * WIN].rearrange("p (b j) -> p b j", b=NB)
            new = s_mask[0:NS, NB * WIN:].rearrange("p (b l) -> p b l", b=NB)
            where(cache, [[-L, NB], [0, WIN]], 0, 1, ALU.is_ge, NEG)
            where(cache, [[L, NB], [0, WIN]], L - 1, -1, ALU.is_ge, NEG)
            where(cache, [[L, NB], [1, WIN]], -1, -1, ALU.is_ge, NEG)
            where(new, [[-L, NB], [0, L]], 0, 1, ALU.is_ge, NEG)
            where(new, [[L, NB], [0, L]], L - 1, -1, ALU.is_ge, NEG)
            where(new, [[-L, NB], [-1, L]], 0, 1, ALU.is_ge, NEG)
            pool.sem_inc(mask_s_made, 1)
            barrier(pool, 2)
            barrier(pool, 3)
            barrier(pool, 4)
            link(pool.iota(part_i, pattern=[[1, TOPK]], base=0, channel_multiplier=0))
            link(pool.tensor_copy(iota16, part_i))
            link(pool.memset(keys_bd[:, :, :], 0.0))
            link(pool.memset(zeros_bf, 0.0))
            link(pool.memset(zmov_bf, 0.0))
            pool.sem_inc(e_consts, 1)
            with pool.Fori(0, NT) as t:
                with pool.Fori(0, PH // 2) as hp:
                    for par in range(2):
                        n = t * PH + hp * 2 + par
                        hold(pool, "pool", idx_made, n + 1)
                        for k in range(TOPK):
                            hold(pool, "pool", u_free, n * TOPK + k + 1)
                            pool.indirect_dma_start(out=u_ring[k % RING][:, :], out_offset=None, in_=eu,
                                                    in_offset=bass.IndirectOffsetOnAxis(ap=idx[par][:, k:k + 1], axis=0)
                                                    ).then_inc(u_in[k % RING], 16)
                        for k in range(TOPK):
                            hold(pool, "pool", v_free, n * TOPK + k + 1)
                            pool.indirect_dma_start(out=v_ring[k % RING][:, :], out_offset=None, in_=ev,
                                                    in_offset=bass.IndirectOffsetOnAxis(ap=idx[par][:, k:k + 1], axis=0)
                                                    ).then_inc(v_in[k % RING], 16)
            base = NT * PH * TOPK
            for h in range(PH):
                pool.wait_ge(idx_s_made, h + 1)
                for k in range(4):
                    r = (4 * h + k) % RING
                    pool.wait_ge(u_free, base + 4 * h + k + 1)
                    pool.indirect_dma_start(out=u_ring[r][:, :], out_offset=None, in_=eu,
                                            in_offset=bass.IndirectOffsetOnAxis(ap=idx_s[h % 2][:, k:k + 1], axis=0)
                                            ).then_inc(u_in[r], 16)
                for k in range(4):
                    r = (4 * h + k) % RING
                    pool.wait_ge(v_free, base + 4 * h + k + 1)
                    pool.indirect_dma_start(out=v_ring[r][:, :], out_offset=None, in_=ev,
                                            in_offset=bass.IndirectOffsetOnAxis(ap=idx_s[h % 2][:, k:k + 1], axis=0)
                                            ).then_inc(v_in[r], 16)

        @block.scalar
        def _(act):
            link = Chain(act, chain_act)
            act.wait_ge(small_in, 16 * 6)
            nc.scalar.activation(ec9[0:NB + 1, :], c9[0:NB + 1, :], ACT.Exp, scale=-1.0).then_inc(exp_c, 1)
            act.wait_ge(ada_free, NBLK + ARING)
            act.dma_start(mod_p, mod9[NB:NB + 1, :]).then_inc(mod_stored, 16)
            for l in range(L):
                act.dma_start(mod_s.rearrange("(b l) n -> l b n", l=L)[l], mod9[0:NB, :]).then_inc(mod_stored, 16)
            act.wait_ge(mod_stored, 16 * (1 + L))
            barrier(act, 0)

            def token_rms(x, out_sq, s, r, parts):
                link(nc.scalar.activation(out_sq[0:parts, :], x[0:parts, :], ACT.Square, accum_out=s[0:parts, :]))
                return nc.scalar.activation(r[0:parts, :], s[0:parts, :], ACT.Sqrt, scale=1.0 / D, bias=eps[0:parts, :])

            act.wait_ge(scale1_made, 1)
            with act.Fori(0, NT // 2) as i:
                for u in range(2):
                    t = i * 2 + u
                    hold(act, "act", x_in[u], i * 16 + 16)
                    link.note(token_rms(xt[u], junk, ssq, rms, P))
                    link.settle()
                    act.sem_inc(rms_made, 1)
                    hold(act, "act", hT_ps, t + 1)
                    hold(act, "act", hT_kept, t + 1)
                    link(nc.scalar.copy(hT_now[:, :, :].rearrange("p k t -> p (k t)"), banks(0, 2)))
                    act.sem_inc(hT_copied, 1)
                    hold(act, "act", qkv_ps, t * 3 + 3)
                    hold(act, "act", v_placed, t + 1)
                    link(nc.scalar.copy(qkv[:, :], banks(0, 3)))
                    act.sem_inc(qkv_out, 1)
                    link(nc.scalar.activation(sq[:, :, :].rearrange("p h d -> p (h d)"), qkv[:, 0:D + KVW], ACT.Square))
                    act.sem_inc(hss_made, 1)
                    hold(act, "act", hss_made, t * 2 + 2)
                    link(nc.scalar.activation(hrms[:, :], hss[:, :], ACT.Sqrt, scale=1.0 / HD, bias=eps[:, :]))
                    act.sem_inc(hrms_made, 1)
                    hold(act, "act", qkT_ps, t + 1)
                    link(nc.scalar.copy(qT_now[:, :, :].rearrange("p k t -> p (k t)"), banks(0, 2)))
                    act.sem_inc(qT_made, 1)
                    for g in range(NKV):
                        hold(act, "act", max_made, t * 4 + (g + 1))
                        for h in range(4):
                            link.note(nc.scalar.activation(pe_[:, h, :], sm[:, h, :], ACT.Exp, bias=nmax[:, h:h + 1],
                                                           accum_out=den[:, h:h + 1]))
                        link(nc.scalar.activation(esink[:, :], sdif[:, :], ACT.Exp))
                        act.sem_inc(exp_made, 1)
                        hold(act, "act", den_made, t * 4 + (g + 1))
                        for h in range(4):
                            link.note(nc.scalar.activation(pe_[:, h, :], pe_[:, h, :], ACT.Copy, scale=rden[:, h:h + 1]))
                        link.settle()
                        act.sem_inc(p_made, 1)
                        hold(act, "act", pT_ps, t * 4 + (g + 1))
                        hold(act, "act", pv_ps, t * 4 + (g + 4))
                        link(nc.scalar.copy(pT[:, 0, :, :].rearrange("p h t -> p (h t)"), banks(5, 1)))
                        act.sem_inc(pT0_made, 1)
                link.restart()
            barrier(act, 1)
            act.wait_ge(sx_in, 16)
            link(token_rms(xt[0], junk, ssq, rms, NS))
            act.sem_inc(s_act, 1)
            act.wait_ge(s_pe, 1)
            link(nc.scalar.copy(hT[:, :, NP:T], banks(0, 1)[:, 0:KC * NS].rearrange("p (k t) -> p k t", k=KC)))
            act.sem_inc(s_act, 1)
            act.wait_ge(s_kcps, 1)
            for e in range(2):
                for half in range(2):
                    link.note(nc.scalar.copy(kcT[HD * half:HD * half + HD, e, 0:NB * WIN],
                                             banks(3, 2)[HD * e:HD * e + HD, :]))
            link.settle()
            act.sem_inc(s_kc0, 1)
            act.wait_ge(s_pe, 2)
            link(nc.scalar.copy(qkv[0:NS, :], banks(0, 3)[0:NS, :]))
            act.sem_inc(s_act, 1)
            link(nc.scalar.activation(sq[0:NS, :, :].rearrange("p h d -> p (h d)"), qkv[0:NS, 0:D + KVW], ACT.Square))
            act.sem_inc(s_act, 1)
            act.wait_ge(s_dve, 2)
            link(nc.scalar.activation(hrms[0:NS, :], hss[0:NS, :], ACT.Sqrt, scale=1.0 / HD, bias=eps[0:NS, :]))
            act.sem_inc(s_act, 1)
            for g in range(NKV):
                act.wait_ge(s_dve, 5 + 4 * g)
                link(nc.scalar.activation(s_sm[:, :], s_sm[:, :], ACT.Exp, bias=nmax[:, 0:1], accum_out=den[:, 0:1]))
                link(nc.scalar.activation(esink[:, 0:1], sdif[:, 0:1], ACT.Exp))
                act.sem_inc(s_act, 1)
                act.wait_ge(s_dve, 6 + 4 * g)
                link(nc.scalar.activation(s_sm[:, :], s_sm[:, :], ACT.Copy, scale=rden[:, 0:1]))
                act.sem_inc(s_act, 1)
            barrier(act, 2)
            link.restart()
            with act.Fori(0, KC // 2) as i:
                for j in range(2):
                    b_u, b_gc, b_ga = (3 * ((5 * j + n) % 2) for n in (0, 3, 4))
                    hold(act, "act", conv_ps, i * 10 + (5 * j + 1))
                    hold(act, "act", cu_made, i * 2 + (j + 1))
                    link(nc.scalar.copy(u_sb[:, :], banks(b_u, 3)[:, 0:T]))
                    act.sem_inc(conv_read, 1)
                    act.sem_inc(u_made, 1)
                    hold(act, "act", conv_ps, i * 10 + (5 * j + 4))
                    hold(act, "act", conv_read, i * 10 + (5 * j + 5))
                    link(nc.scalar.activation(sg_c[:, :], banks(b_gc, 3)[:, 0:T], ACT.Sigmoid))
                    act.sem_inc(conv_read, 1)
                    act.sem_inc(gate_c_made, 1)
                    hold(act, "act", conv_ps, i * 10 + (5 * j + 5))
                    link(nc.scalar.activation(sg_a[:, :], banks(b_ga, 3)[:, 0:T], ACT.Sigmoid))
                    act.sem_inc(conv_read, 1)
                    act.sem_inc(gate_a_made, 1)
                link.restart()
            barrier(act, 3)
            act.wait_ge(new_ps, 1)
            act.sem_inc(qry_kept, 1)
            link(nc.scalar.copy(junk2[0:2 + NB * 2, :], banks(0, 2)[0:2 + NB * 2, :]))
            act.dma_start(new_conv_prompt.rearrange("a b r d -> (a b r) d"), junk2[0:2, :]).then_inc(new_stored, 16)
            act.dma_start(new_conv_sample.rearrange("a b r d -> (a b r) d"), junk2[2:2 + NB * 2, :]).then_inc(new_stored, 16)
            act.wait_ge(new_stored, 32)
            act.sem_inc(new_made, 1)
            link.restart()

            def d_tile(wait, t, parts, x2_at, h2_at, q_at):
                wait(x2_made, t + 1)
                link(token_rms(x2, junk2, ssq2, rms2, parts))
                act.sem_inc(rms2_made, 1)
                act.dma_start(x2_at, x2[0:parts, :]).then_inc(x2h2_stored, 16)
                wait(h2_made, t + 1)
                act.dma_start(h2_at, h2[0:parts, :]).then_inc(x2h2_stored, 16)
                wait(h2T_ps, t + 1)
                link(nc.scalar.copy(h2T[:, :, 0:parts], banks(2, 2).rearrange("p (k t) -> p k t", k=KC)[:, :, 0:parts]))
                act.sem_inc(h2T_made, 1)
                wait(qry_ps, t + 1)
                link(nc.scalar.copy(q_at, banks(4, 2).rearrange("p (h t) -> p h t", h=PH)[:, :, 0:parts]))
                act.sem_inc(qry_kept, 1)

            with act.Fori(0, NT) as t:
                d_tile(lambda s, v: hold(act, "act", s, v), t, P,
                       x2_d[bass.ds(t, 1), :, :].rearrange("a p d -> (a p) d"),
                       h2_d[bass.ds(t, 1), :, :].rearrange("a p d -> (a p) d"),
                       query_t[:, bass.ds(t * (PH * P), PH * P)].rearrange("p (h t) -> p h t", h=PH))
                link.restart()
            d_tile(act.wait_ge, NT, NS, x2_d[NT, 0:NS, :], h2_d[NT, 0:NS, :],
                   query_t[:, NT * PH * P:].rearrange("p (h t) -> p h t", h=PH)[:, :, 0:NS])
            act.wait_ge(x2h2_stored, 32 * (NT + 1))
            barrier(act, 4)
            link.restart()

            def stage_query(wait, n, par):
                wait(s_ps, n)
                link(nc.scalar.copy(q_st[par][:, :], query_t[:, bass.ds(n * P, P)]))
                act.sem_inc(q_staged, 1)
                wait(s_ps, n + 1)
                link(nc.scalar.copy(s_sb[par][:, :, :].rearrange("p c n -> p (c n)"), banks(4, 1)[:, 0:2 * PK]))
                act.sem_inc(s_out, 1)

            def gate_exps(wait, n):
                wait(best_made, n + 1)
                link(nc.scalar.activation(gate_e[:, :], best_v[:, :], ACT.Exp, bias=nbest[:, :], accum_out=gsum[:, :]))
                act.sem_inc(gate_exp, 1)

            act.wait_ge(e_keys_made, 1)
            link(nc.scalar.copy(q_st[0][:, :], query_t[:, 0:P]))
            act.sem_inc(q_staged, 1)
            act.wait_ge(s_ps, 1)
            link(nc.scalar.copy(s_sb[0][:, :, :].rearrange("p c n -> p (c n)"), banks(4, 1)[:, 0:2 * PK]))
            act.sem_inc(s_out, 1)
            gate_exps(act.wait_ge, 0)
            link.restart()

            def reg(s, v):
                hold(act, "act", s, v)

            with act.Fori(0, NT) as t:
                with act.Fori(0, PH // 2) as hp:
                    for par in range(2):
                        n = t * PH + hp * 2 + par
                        stage_query(reg, n + 1, 1 - par)
                        reg(u_free, n * TOPK + (RING + TOPK))
                        link(nc.scalar.activation(act_dot[:, :], dot[:, :], ACT.Gelu))
                        act.sem_inc(gelu_made, 1)
                        reg(wgt_made, n + 1)
                        for k in range(TOPK):
                            reg(v_free, n * TOPK + (k + 1))
                            nc.scalar.activation(diag[k % RING][:, :], ident[:, :], ACT.Copy, scale=wgt[:, k:k + 1]
                                                 ).then_inc(diag_made, 1)
                        gate_exps(reg, n + 1)
                    link.restart()
            base = NT * PH * TOPK
            for h in range(PH):
                n = NT * PH + h
                if h + 1 < PH:
                    stage_query(act.wait_ge, n + 1, (h + 1) % 2)
                act.wait_ge(u_free, RING + base + 4 * (h + 1))
                link(nc.scalar.activation(act_dot[:, 0:4], dot[:, 0:4], ACT.Gelu))
                act.sem_inc(gelu_made, 1)
                act.wait_ge(wgt_made, n + 1)
                for k in range(4):
                    act.wait_ge(v_free, base + 4 * h + k + 1)
                    nc.scalar.activation(diag[(4 * h + k) % RING][:, 0:NS], sel_s[:, :], ACT.Copy, scale=wgt[:, k:k + 1]
                                         ).then_inc(diag_made, 1)
                if h + 1 < PH:
                    gate_exps(act.wait_ge, n + 1)

        @block.vector
        def _(dve):
            link = Chain(dve, chain_dve)
            V = nc.vector

            def reg(s, v):
                hold(dve, "dve", s, v)

            dve.wait_ge(exp_c, 1)
            link(V.tensor_scalar(ec9[0:NB + 1, :], ec9[0:NB + 1, :], 1.0, None, ALU.add))
            link(V.reciprocal(ec9[0:NB + 1, :], ec9[0:NB + 1, :]))
            link(V.tensor_tensor(c9[0:NB + 1, :], c9[0:NB + 1, :], ec9[0:NB + 1, :], ALU.mult))
            dve.sem_inc(silu_made, 1)
            dve.wait_ge(small_ps, 1)
            small = banks(6, 1)
            link.note(V.tensor_copy(cT[:, :, :], small[:, 0:72].rearrange("p (k c) -> p k c", k=KC)))
            link.note(V.tensor_copy(state_t[:, :, :], small[:, 72:200].rearrange("p (k c) -> p k c", k=KC)))
            link(V.tensor_copy(cw[:, :, :], small[:, 200:232].rearrange("p (k c) -> p c k", k=KC)))
            dve.sem_inc(small_made, 1)
            dve.sem_inc(ada_free, ARING)
            with dve.Fori(0, NBLK // ARING) as j:
                for r in range(ARING):
                    reg(ada_ps, j * ARING + r + 1)
                    cols = bass.ds(j * (ARING * ABLK) + r * ABLK, ABLK)
                    V.tensor_tensor(mod9[0:NB + 1, cols], banks(r, 1)[0:NB + 1, :], bada9[0:NB + 1, cols],
                                    ALU.add).then_inc(ada_free, 1)
            barrier(dve, 0)

            def first_norm(x, a, b, h, r, rs, parts):
                link(V.reciprocal(rs[0:parts, :], r[0:parts, :]))
                link(V.scalar_tensor_tensor(out=h[0:parts, :], in0=x[0:parts, :], scalar=rs[0:parts, :],
                                            in1=a[0:parts, :], op0=ALU.mult, op1=ALU.mult))
                link(V.tensor_tensor(h[0:parts, :], h[0:parts, :], b[0:parts, :], ALU.add))

            def head_norm(parts):
                link(V.reciprocal(hrs[0:parts, :], hrms[0:parts, :]))
                heads = qkv[0:parts, 0:D + KVW].rearrange("p (h d) -> p h d", h=NQK)
                link(V.tensor_tensor(heads, heads, hrs[0:parts, :].unsqueeze(2).to_broadcast([parts, NQK, HD]), ALU.mult))
                link(V.tensor_tensor(heads, heads, qk_w[0:parts, :, :], ALU.mult))

            dve.wait_ge(rows_in, 16 * 8)
            for n, parts in ((0, P), (1, NS)):
                link(V.scalar_tensor_tensor(out=A1[n][0:parts, :], in0=A1[n][0:parts, :], scalar=1.0,
                                            in1=junk[0:parts, :], op0=ALU.add, op1=ALU.mult))
            link.note(V.tensor_copy(qk_w[:, 1:NH, :], qk_w[:, 0:1, :].to_broadcast([P, NH - 1, HD])))
            link(V.tensor_copy(qk_w[:, NH + 1:NQK, :], qk_w[:, NH:NH + 1, :].to_broadcast([P, NKV - 1, HD])))
            dve.sem_inc(scale1_made, 1)
            dve.sem_inc(x_free, 2)
            dve.sem_inc(score_read, 1)
            dve.sem_inc(o_kept, 1)
            dve.sem_inc(v_placed, 1)
            dve.sem_inc(hT_kept, 1)
            dve.wait_ge(attn_zeroed, 1)
            link.restart()
            with dve.Fori(0, NT // 2) as i:
                for u in range(2):
                    t = i * 2 + u
                    reg(rms_made, t + 1)
                    first_norm(xt[u], A1[0], B1[0], h_row, rms, rstd, P)
                    dve.sem_inc(x_free, 1)
                    dve.sem_inc(h_made, 1)
                    reg(hss_made, t * 2 + 1)
                    link(V.tensor_reduce(hss[:, :], sq[:, :, :], AX.X, ALU.add))
                    dve.sem_inc(hss_made, 1)
                    reg(hrms_made, t + 1)
                    head_norm(P)
                    dve.sem_inc(qk_normed, 1)
                    reg(qkT_ps, t + 1)
                    kT = banks(2, 1)[:, 0:2 * P].rearrange("p (c t) -> p c t", c=2)
                    for e in range(2):
                        for half in range(2):
                            link.note(V.tensor_copy(
                                kpad[HD * half:HD * half + HD, :, half, u, :].rearrange("p (c e) t -> p c e t", e=2)[:, :, e, :],
                                kT[HD * e:HD * e + HD, :, :]))
                    link.settle()
                    dve.sem_inc(kpad_made, 1)
                    for g in range(NKV):
                        reg(score_ps, t * 4 + (g + 1))
                        link(V.scalar_tensor_tensor(
                            out=sm[:, :, :], in0=banks(3, 2).rearrange("p (h n) -> p h n", h=4), scalar=SCALE,
                            in1=maskt[:, u, :, :].rearrange("p s n -> p (s n)").unsqueeze(1).to_broadcast([P, 4, 2 * P]),
                            op0=ALU.mult, op1=ALU.add))
                        dve.sem_inc(score_read, 1)
                        link(V.tensor_reduce(smax[:, :], sm[:, :, :], AX.X, ALU.max))
                        sink_g = sink_row[:, 4 * g:4 * g + 4]
                        link(V.tensor_tensor(smax[:, :], smax[:, :], sink_g, ALU.max))
                        link.note(V.tensor_scalar(nmax[:, :], smax[:, :], -1.0, None, ALU.mult))
                        link(V.tensor_tensor(sdif[:, :], sink_g, smax[:, :], ALU.subtract))
                        dve.sem_inc(max_made, 1)
                        reg(exp_made, t * 4 + (g + 1))
                        link(V.tensor_tensor(den[:, :], den[:, :], esink[:, :], ALU.add))
                        link(V.reciprocal(rden[:, :], den[:, :]))
                        dve.sem_inc(den_made, 1)
                        reg(pT_ps, t * 4 + (g + 1))
                        reg(pv_ps, t * 4 + (g + 4))
                        link(V.tensor_copy(pT[:, 1, :, :].rearrange("p h t -> p (h t)"), banks(6, 1)))
                        dve.sem_inc(pT1_made, 1)
                        if g % 2:
                            reg(pv_ps, t * 4 + (g + 5))
                            link(V.tensor_copy(oT[:, 2 * (g - 1):2 * (g - 1) + 4, bass.ds(t * P, P)],
                                               banks(7, 1).rearrange("p (c t) -> p c t", c=4)))
                            dve.sem_inc(o_kept, 1)
                    if u == 0:
                        link(V.tensor_copy(maskt[:, 0, :, :], maskt[:, 2, :, :]))
                link.restart()
            barrier(dve, 1)
            dve.wait_ge(s_act, 1)
            first_norm(xt[0], A1[1], B1[1], h_row, rms, rstd, NS)
            dve.sem_inc(s_dve, 1)
            dve.wait_ge(s_kcps, 2)
            for e in range(2):
                for half in range(2):
                    link.note(V.tensor_copy(kcT[HD * half:HD * half + HD, 2 + e, 0:NB * WIN],
                                            banks(5, 2)[HD * e:HD * e + HD, :]))
            link.settle()
            dve.sem_inc(s_kc1, 1)
            dve.wait_ge(s_act, 4)
            link(V.tensor_reduce(hss[0:NS, :], sq[0:NS, :, :], AX.X, ALU.add))
            dve.sem_inc(s_dve, 1)
            dve.wait_ge(s_act, 5)
            head_norm(NS)
            dve.sem_inc(s_dve, 1)
            dve.wait_ge(mask_s_made, 1)
            for q in range(1, 4):
                link.note(V.tensor_copy(s_mask[32 * q:32 * q + 32, :], s_mask[0:NS, :]))
            dve.wait_ge(s_pe, 3)
            qs = banks(0, 1)[:, 0:KC * NS].rearrange("p (g r t) -> p g r t", g=NKV, r=2)
            ks = banks(0, 1)[:, KC * NS:(KC + 2) * NS].rearrange("p (c t) -> p c t", c=2)
            for half in range(2):
                for g in range(NKV):
                    link.note(V.tensor_copy(qz[HD * half:HD * half + HD, g, :, half, :], qs[HD * half:HD * half + HD, g, :, :]))
                for e in range(2):
                    link.note(V.tensor_copy(
                        kcT[HD * half:HD * half + HD, :, NB * WIN:].rearrange("p (c e) t -> p c e t", e=2)[:, :, e, :],
                        ks[HD * e:HD * e + HD, :, :]))
            link.settle()
            dve.wait_ge(s_rows, 64)
            dve.sem_inc(s_dve, 1)
            for g in range(NKV):
                dve.wait_ge(s_pe, 4 + 3 * g)
                link(V.scalar_tensor_tensor(out=s_sm[:, :], in0=banks(3, 3)[:, 0:NB * WIN + NS], scalar=SCALE,
                                            in1=s_mask[:, :], op0=ALU.mult, op1=ALU.add))
                link(V.tensor_reduce(smax[:, 0:1], s_sm[:, :], AX.X, ALU.max))
                link(V.tensor_tensor(smax[:, 0:1], smax[:, 0:1], sink_col[:, g:g + 1], ALU.max))
                link.note(V.tensor_scalar(nmax[:, 0:1], smax[:, 0:1], -1.0, None, ALU.mult))
                link(V.tensor_tensor(sdif[:, 0:1], sink_col[:, g:g + 1], smax[:, 0:1], ALU.subtract))
                dve.sem_inc(s_dve, 1)
                dve.wait_ge(s_act, 6 + 2 * g)
                link(V.tensor_tensor(den[:, 0:1], den[:, 0:1], esink[:, 0:1], ALU.add))
                link(V.reciprocal(rden[:, 0:1], den[:, 0:1]))
                dve.sem_inc(s_dve, 1)
                dve.wait_ge(s_pe, 5 + 3 * g)
                link.note(V.tensor_copy(s_pT[:, 0:NB, :].rearrange("p b t -> p (b t)"), banks(0, 2)))
                link(V.tensor_copy(s_pT[0:NS, NB, :], banks(2, 1)[0:NS, 0:P]))
                dve.sem_inc(s_dve, 1)
                dve.wait_ge(s_pe, 6 + 3 * g)
                e = g % 2
                o_s = banks(6, 1)[HD * e:HD * e + HD, 0:P].rearrange("p (r e t) -> p r e t", r=2, e=2)
                for half in range(2):
                    link.note(V.tensor_copy(oT[HD * half:HD * half + HD, 2 * g:2 * g + 2, NP:T], o_s[:, :, half, :]))
                link.settle()
                dve.sem_inc(s_dve, 1)
            barrier(dve, 2)
            dve.sem_inc(conv_read, 2)
            dve.sem_inc(cu_made, 1)
            link(V.memset(cu_p[:, 0:2], 0.0))
            link.restart()
            with dve.Fori(0, KC // 2) as i:
                for j in range(2):
                    c = i * 2 + j
                    b_pre, b_post = (3 * ((5 * j + n) % 2) for n in (1, 2))
                    link.note(V.tensor_copy(cw_now[:, :], cw[:, :, bass.ds(c, 1)].rearrange("p f c -> p (f c)")))
                    link.note(V.tensor_copy(cu_s[:, :, 0:2], state_t[:, bass.ds(c, 1), :].rearrange("p c (b r) -> p (c b) r", b=NB)))
                    reg(u_made, c + 1)
                    reg(conv_ps, i * 10 + (5 * j + 2))
                    pre = banks(b_pre, 3)
                    link.note(V.tensor_tensor(cu_p[:, 2:], pre[:, 0:NP], u_sb[:, 0:NP], ALU.mult))
                    link(V.tensor_tensor(cu_s[:, :, 2:], pre[:, NP:T].rearrange("p (b l) -> p b l", b=NB),
                                         u_sb[:, NP:T].rearrange("p (b l) -> p b l", b=NB), ALU.mult))
                    dve.sem_inc(conv_read, 1)
                    dve.sem_inc(cu_made, 1)
                    link.note(V.tensor_copy(new_t[:, bass.ds(c, 1), 0:2].rearrange("p c r -> p (c r)"), cu_p[:, NP:NP + 2]))
                    link.note(V.tensor_copy(new_t[:, bass.ds(c, 1), 2:].rearrange("p c (b r) -> p (c b) r", b=NB),
                                            cu_s[:, :, L:L + 2]))
                    y_p, y_s = y_c[:, 0:NP], y_c[:, NP:T].rearrange("p (b l) -> p b l", b=NB)
                    link.note(V.tensor_scalar(y_p, cu_p[:, 0:NP], cw_now[:, 0:1], cw_now[:, 3:4], ALU.mult, ALU.add))
                    link(V.tensor_scalar(y_s, cu_s[:, :, 0:L], cw_now[:, 0:1], cw_now[:, 3:4], ALU.mult, ALU.add))
                    for tap in (1, 2):
                        link.note(V.scalar_tensor_tensor(out=y_p, in0=cu_p[:, tap:tap + NP], scalar=cw_now[:, tap:tap + 1],
                                                         in1=y_p, op0=ALU.mult, op1=ALU.add))
                        link(V.scalar_tensor_tensor(out=y_s, in0=cu_s[:, :, tap:tap + L], scalar=cw_now[:, tap:tap + 1],
                                                    in1=y_s, op0=ALU.mult, op1=ALU.add))
                    reg(conv_ps, i * 10 + (5 * j + 3))
                    link(V.tensor_tensor(y_c[:, :], banks(b_post, 3)[:, 0:T], y_c[:, :], ALU.mult))
                    dve.sem_inc(conv_read, 1)
                    reg(gate_c_made, c + 1)
                    link(V.tensor_tensor(y_c[:, :], y_c[:, :], sg_c[:, :], ALU.mult))
                    reg(gate_a_made, c + 1)
                    o_c = oT[:, bass.ds(c, 1), :].rearrange("p c t -> p (c t)")
                    link(V.tensor_tensor(mg[:, :], o_c, sg_a[:, :], ALU.mult))
                    link(V.tensor_tensor(o_c, mg[:, :], y_c[:, :], ALU.add))
                link.restart()
            barrier(dve, 3)
            dve.wait_ge(d_rows, 64)
            link(V.scalar_tensor_tensor(out=A2[:, :], in0=A2[:, :], scalar=1.0, in1=n2[:, :], op0=ALU.add, op1=ALU.mult))
            link(V.memset(query_t[:, NT * PH * P:], 0.0))
            dve.sem_inc(rows_made, 1)
            dve.sem_inc(xd_free, 2)
            link.restart()

            def d_tile(wait, t, parts, merged, x, x_wait):
                link(V.tensor_copy(mT[:, :, 0:parts], merged))
                dve.sem_inc(mT_made, 1)
                wait(out_ps, t + 1)
                if x_wait is not None:
                    wait(*x_wait)
                link(V.tensor_tensor(x2[0:parts, :], banks(0, 2)[0:parts, :], G1[0:parts, :], ALU.mult))
                link(V.tensor_tensor(x2[0:parts, :], x2[0:parts, :], x[0:parts, :], ALU.add))
                dve.sem_inc(x2_made, 1)
                dve.sem_inc(xd_free, 1)
                wait(rms2_made, t + 1)
                first_norm(x2, A2, B2, h2, rms2, rstd2, parts)
                dve.sem_inc(h2_made, 1)
                wait(h2T_ps, t + 1)
                wait(x2h2_stored, t * 32 + 32)

            with dve.Fori(0, NT // 2) as i:
                for u in range(2):
                    t = i * 2 + u
                    d_tile(reg, t, P, oT[:, :, bass.ds(t * P, P)], xd[u], (xd_in[u], i * 16 + 16))
                link.restart()
            dve.wait_ge(d_rows, 64 + 48)
            dve.wait_ge(xd_in[0], 16 * (NT // 2 + 1))
            link(V.scalar_tensor_tensor(out=A2[0:NS, :], in0=A2[0:NS, :], scalar=1.0, in1=n2[0:NS, :], op0=ALU.add, op1=ALU.mult))
            d_tile(dve.wait_ge, NT, NS, oT[:, :, NP:T], xd[0], None)
            barrier(dve, 4)
            dve.wait_ge(e_consts, 1)
            dve.wait_ge(e_keys_ps, 1)
            kps = banks(0, 2).rearrange("p (h n) -> p h n", h=PH)
            for c in range(2):
                link.note(V.tensor_copy(keys_bd[HD * c:HD * c + HD, 0:PH, PK * c:PK * c + PK], kps[HD * c:HD * c + HD, :, :]))
                link.note(V.tensor_copy(keys_bd[HD * c:HD * c + HD, PH, PK * c:PK * c + PK], kps[HD * c:HD * c + HD, 0, :]))
            link.settle()
            dve.sem_inc(e_keys_made, 1)
            dve.sem_inc(u_free, RING)
            dve.sem_inc(v_free, RING)
            dve.sem_inc(y_read, 1)

            def top16(values, cut, out_v, out_i):
                link(V.max(out_v[:, 0:8], values))
                link.note(V.max_index(out_i[:, 0:8], out_v[:, 0:8], values))
                link(V.match_replace(cut, out_v[:, 0:8], values, LOWEST))
                link(V.max(out_v[:, 8:16], cut))
                link(V.max_index(out_i[:, 8:16], out_v[:, 8:16], cut))

            def pick(wait, n, par):
                wait(s_out, n + 1)
                for c in range(2):
                    top16(s_sb[par][:, c, :], s_cut[:, :], top_v[:, c, :], top_i[:, c, :])
                link.note(V.tensor_copy(top_f[:, :, :], top_i[:, :, :]))
                link(V.tensor_tensor(cand[:, :, :], top_v[:, 0, :].unsqueeze(2).to_broadcast([P, TOPK, TOPK]),
                                     top_v[:, 1, :].unsqueeze(1).to_broadcast([P, TOPK, TOPK]), ALU.add))
                top16(cand[:, :, :].rearrange("p a b -> p (a b)"), cand_cut[:, :, :].rearrange("p a b -> p (a b)"),
                      best_v[:, :], best_i[:, :])
                link(V.tensor_scalar(nbest[:, :], best_v[:, 0:1], -1.0, None, ALU.mult))
                dve.sem_inc(best_made, 1)
                for c, (op, arg) in enumerate(((ALU.logical_shift_right, 4), (ALU.bitwise_and, TOPK - 1))):
                    link(V.tensor_scalar(part_i[:, :], best_i[:, :], arg, None, op))
                    link(V.tensor_copy(best_f[:, :], part_i[:, :]))
                    link(V.tensor_tensor(onehot[:, :, :], best_f[:, :].unsqueeze(2).to_broadcast([P, TOPK, TOPK]),
                                         iota16[:, :].unsqueeze(1).to_broadcast([P, TOPK, TOPK]), ALU.is_equal))
                    link(V.tensor_tensor(onehot[:, :, :], onehot[:, :, :],
                                         top_f[:, c, :].unsqueeze(1).to_broadcast([P, TOPK, TOPK]), ALU.mult))
                    link(V.tensor_reduce(i_half[:, c, :], onehot[:, :, :], AX.X, ALU.add))
                link(V.scalar_tensor_tensor(out=idx[par][:, :], in0=i_half[:, 0, :], scalar=float(PK),
                                            in1=i_half[:, 1, :], op0=ALU.mult, op1=ALU.add))

            def gates(wait, n):
                wait(gate_exp, n + 1)
                link(V.reciprocal(gsum[:, :], gsum[:, :]))
                link(V.tensor_scalar(gate[:, :], gate_e[:, :], gsum[:, :], None, ALU.mult))

            pick(dve.wait_ge, 0, 0)
            dve.sem_inc(idx_made, 1)
            gates(dve.wait_ge, 0)
            dve.wait_ge(e_g2_in, 16)
            link.restart()
            with dve.Fori(0, NT) as t:
                reg(h2_in, t * 16 + 16)
                link(V.tensor_copy(h2_now[:, :], h2_next[:, :]))
                dve.sem_inc(h2_taken, 1)
                link.restart()
                with dve.Fori(0, PH // 2) as hp:
                    for par in range(2):
                        n = t * PH + hp * 2 + par
                        for k in range(TOPK):
                            reg(u_in[k % RING], n * 32 + 16 * (k // RING + 1))
                            reg(u_free, n * TOPK + (RING + k - 1))
                            V.tensor_tensor_reduce(out=prod[:, k % 2, :], in0=u_ring[k % RING][:, :],
                                                   in1=h2_now[:, :], scale=1.0, scalar=0.0, op0=ALU.mult,
                                                   op1=ALU.add, accum_out=dot[:, k:k + 1]).then_inc(u_free, 1)
                        reg(gelu_made, n + 1)
                        reg(v_free, n * TOPK + RING)
                        link(V.tensor_tensor(wgt[:, :], act_dot[:, :], gate[:, :], ALU.mult))
                        dve.sem_inc(wgt_made, 1)
                        pick(reg, n + 1, 1 - par)
                        dve.sem_inc(idx_made, 1)
                        gates(reg, n + 1)
                    link.restart()
                reg(y_ps, t + 1)
                reg(y_free, t + 1)
                link(V.tensor_tensor(y_now[:, :], banks(0, 2), G2[:, :], ALU.mult))
                dve.sem_inc(y_read, 1)
                reg(x2_in, t * 16 + 16)
                link(V.tensor_tensor(y_now[:, :], y_now[:, :], x2_now[:, :], ALU.add))
                dve.sem_inc(y_made, 1)
                link.restart()
            dve.wait_ge(h2_in, 16 * (NT + 4))
            link(V.tensor_copy(h2_now[:, :], h2_next[:, :]))
            base = NT * PH * TOPK

            def pack(h):
                for q in range(4):
                    link.note(V.tensor_copy(idx_s[h % 2][NS * q:NS * q + NS, :], idx[h % 2][0:NS, 4 * q:4 * q + 4]))
                    link.note(V.tensor_copy(gate_s[NS * q:NS * q + NS, :], gate[0:NS, 4 * q:4 * q + 4]))
                link.settle()
                dve.sem_inc(idx_s_made, 1)

            pack(0)
            for h in range(PH):
                n = NT * PH + h
                for k in range(4):
                    m = 4 * h + k
                    dve.wait_ge(u_in[m % RING], 16 * (NT * PH * 2 + m // RING + 1))
                    dve.wait_ge(u_free, RING + base + m - 1)
                    V.tensor_tensor_reduce(out=prod[:, k % 2, :], in0=u_ring[m % RING][:, :], in1=h2_now[:, :], scale=1.0,
                                           scalar=0.0, op0=ALU.mult, op1=ALU.add, accum_out=dot[:, k:k + 1]).then_inc(u_free, 1)
                dve.wait_ge(gelu_made, n + 1)
                dve.wait_ge(v_free, RING + base + 4 * h)
                link(V.tensor_tensor(wgt[:, 0:4], act_dot[:, 0:4], gate_s[:, :], ALU.mult))
                dve.sem_inc(wgt_made, 1)
                if h + 1 < PH:
                    pick(dve.wait_ge, n + 1, (h + 1) % 2)
                    gates(dve.wait_ge, n + 1)
                    pack(h + 1)
            dve.wait_ge(y_ps, NT + 1)
            dve.wait_ge(y_free, NT + 1)
            dve.wait_ge(e_g2_in, 32)
            link(V.tensor_tensor(y_now[0:NS, :], banks(0, 2)[0:NS, :], G2[0:NS, :], ALU.mult))
            dve.wait_ge(x2_in, 16 * (NT + 1))
            link(V.tensor_tensor(y_now[0:NS, :], y_now[0:NS, :], x2_now[0:NS, :], ALU.add))
            dve.sem_inc(y_made, 1)

        @block.tensor
        def _(pe):
            M, TR = nc.tensor.matmul, nc.tensor.transpose

            def reg(s, v):
                hold(pe, "pe", s, v)

            pe.wait_ge(consts_made, 1)
            pe.wait_ge(silu_made, 1)
            small = banks(6, 1)
            for rows, n, at in ((c9, NB + 1, 0), (st16, NB * 2, 72), (cw4, 4, 200)):
                for k in range(KC):
                    last = TR(small[:, at + k * n:at + (k + 1) * n], rows[0:n, k * P:(k + 1) * P], ident[0:n, 0:n])
            last.then_inc(small_ps, 1)
            pe.wait_ge(small_made, 1)
            with pe.Fori(0, NBLK // ARING) as j:
                for r in range(ARING):
                    reg(ada_in[r], j * 16 + 16)
                    reg(ada_free, j * ARING + r + 1)
                    for k in range(KC):
                        last = M(banks(r, 1)[0:NB + 1, :], cT[:, k, :], ada_w[r][:, k, :], start=k == 0, stop=k == KC - 1)
                    last.then_inc(ada_ps, 1)
            pe.wait_ge(qkv_w_in, 16)
            barrier(pe, 0)
            pe.wait_ge(attn_zeroed, 1)
            pe.sem_inc(pv_ps, 4)
            with pe.Fori(0, NT // 2) as i:
                for u in range(2):
                    t = i * 2 + u
                    reg(h_made, t + 1)
                    for k in range(KC):
                        last = TR(banks(0, 2)[:, k * P:(k + 1) * P], h_row[:, k * P:(k + 1) * P], ident[:, :])
                    last.then_inc(hT_ps, 1)
                    reg(hT_copied, t + 1)
                    for c in range(3):
                        for k in range(KC):
                            last = M(banks(c, 1), hT_now[:, k, :], w_qkv[:, k, c * 512:(c + 1) * 512], start=k == 0, stop=k == KC - 1)
                        last.then_inc(qkv_ps, 1)
                    reg(qk_normed, t + 1)
                    for k in range(KC + 2):
                        last = TR(banks(0, 3)[:, k * P:(k + 1) * P], qkv[:, k * P:(k + 1) * P], ident[:, :])
                    last.then_inc(qkT_ps, 1)
                    reg(qT_made, t + 1)
                    reg(kpad_made, t + 1)
                    for g in range(NKV):
                        reg(score_read, t * 4 + (g + 1))
                        for pair in range(2):
                            last = M(banks(3 + pair, 1), qT_now[:, 2 * g + pair, :],
                                     kpad[:, g, :, :, :].rearrange("p e s n -> p (e s n)"), start=True, stop=True)
                        last.then_inc(score_ps, 1)
                        reg(p_made, t * 4 + (g + 1))
                        for s in range(2):
                            for h in range(4):
                                last = TR(banks(5 + s, 1)[:, h * P:(h + 1) * P], pe_[:, h, s * P:(s + 1) * P], ident[:, :])
                        last.then_inc(pT_ps, 1)
                        reg(pT0_made, t * 4 + (g + 1))
                        reg(pT1_made, t * 4 + (g + 1))
                        reg(v_placed, t + 2)
                        if g % 2 == 0:
                            reg(o_kept, t * 2 + (g // 2 + 1))
                        for pair in range(2):
                            at = ((g % 2) * 2 + pair) * P
                            for e in range(2):
                                for s in range(2):
                                    last = M(banks(7, 1)[:, at:at + P], vpad[:, s, g, HD * e:HD * e + P], pT[:, s, 2 * pair + e, :],
                                             start=e == 0 and s == 0, stop=e == 1 and s == 1)
                        last.then_inc(pv_ps, 1)
            barrier(pe, 1)
            pe.wait_ge(scache_in, 32)
            for c in range(2):
                for b in range(NB):
                    last = TR(banks(3 + 2 * c, 2)[:, b * P:(b + 1) * P], ck_sb[:, b, c * P:(c + 1) * P], ident[:, :])
                last.then_inc(s_kcps, 1)
            pe.wait_ge(s_dve, 1)
            for k in range(KC):
                last = TR(banks(0, 1)[:, k * NS:(k + 1) * NS], h_row[0:NS, k * P:(k + 1) * P], ident[0:NS, 0:NS])
            last.then_inc(s_pe, 1)
            pe.wait_ge(s_act, 2)
            for c in range(3):
                for k in range(KC):
                    last = M(banks(c, 1)[0:NS, :], hT[:, k, NP:T], w_qkv[:, k, c * 512:(c + 1) * 512], start=k == 0, stop=k == KC - 1)
            last.then_inc(s_pe, 1)
            pe.wait_ge(s_dve, 3)
            for k in range(KC + 2):
                last = TR(banks(0, 1)[:, k * NS:(k + 1) * NS], qkv[0:NS, k * P:(k + 1) * P], ident[0:NS, 0:NS])
            last.then_inc(s_pe, 1)
            pe.wait_ge(s_kc0, 1)
            pe.wait_ge(s_kc1, 1)
            for g in range(NKV):
                pe.wait_ge(s_dve, 4 + 4 * g)
                for at, w in ((0, 512), (512, 512), (1024, NS)):
                    last = M(banks(3, 3)[:, at:at + w], qz[:, g, :, :, :].rearrange("p r e t -> p (r e t)"),
                             kcT[:, g, at:at + w], start=True, stop=True)
                last.then_inc(s_pe, 1)
                pe.wait_ge(s_act, 7 + 2 * g)
                for b in range(NB):
                    TR(banks(0, 2)[:, b * P:(b + 1) * P], s_sm[:, b * P:(b + 1) * P], ident[:, :])
                last = TR(banks(2, 1)[0:NS, 0:P], s_sm[:, NB * P:NB * P + NS], ident[:, :])
                last.then_inc(s_pe, 1)
                pe.wait_ge(s_dve, 7 + 4 * g)
                pair = P * (g // 2)
                for b in range(NB):
                    M(banks(6, 1)[:, 0:P], cv_sb[:, b, pair:pair + P], s_pT[:, b, :], start=b == 0, stop=False)
                last = M(banks(6, 1)[:, 0:P], qkv[0:NS, D + KVW + pair:D + KVW + pair + P], s_pT[0:NS, NB, :], start=False, stop=True)
                last.then_inc(s_pe, 1)
            barrier(pe, 2)
            pe.sem_inc(wc_free, 5)
            with pe.Fori(0, KC // 2) as i:
                for n in range(10):
                    reg(wc_in[n % 5], i * 32 + 16 * (n // 5 + 1))
                    reg(conv_read, i * 10 + (n + 1))
                    b = 3 * (n % 2)
                    for k in range(KC):
                        for at, w in ((0, 512), (512, 512), (1024, NS)):
                            last = M(banks(b, 3)[:, at:at + w], w_c[n % 5][:, k, :], hT[:, k, at:at + w],
                                     start=k == 0, stop=k == KC - 1)
                    last.then_inc(conv_ps, 1)
                    reg(conv_ps, i * 10 + (n + 1))
                    pe.sem_inc(wc_free, 1)
            barrier(pe, 3)
            for k in range(KC):
                last = TR(banks(0, 2)[0:2 + NB * 2, k * P:(k + 1) * P], new_t[:, k, :], ident[:, :])
            last.then_inc(new_ps, 1)
            pe.wait_ge(new_made, 1)
            pe.wait_ge(d_w_in, 32)

            def d_tile(wait, t, parts):
                wait(mT_made, t + 1)
                for c in range(2):
                    for k in range(KC):
                        last = M(banks(c, 1)[0:parts, :], mT[:, k, 0:parts], wo_sb[:, k, c * 512:(c + 1) * 512],
                                 start=k == 0, stop=k == KC - 1)
                last.then_inc(out_ps, 1)
                wait(h2_made, t + 1)
                for k in range(KC):
                    last = TR(banks(2, 2)[:, k * P:k * P + parts], h2[0:parts, k * P:(k + 1) * P], ident[0:parts, 0:parts])
                last.then_inc(h2T_ps, 1)
                wait(h2T_made, t + 1)
                wait(qry_kept, t + 1)
                for h in range(PH):
                    for k in range(KC):
                        last = M(banks(4, 2)[:, h * P:h * P + parts], wq_sb[:, k, h * P:(h + 1) * P], h2T[:, k, 0:parts],
                                 start=k == 0, stop=k == KC - 1)
                last.then_inc(qry_ps, 1)

            with pe.Fori(0, NT) as t:
                d_tile(reg, t, P)
            d_tile(pe.wait_ge, NT, NS)
            barrier(pe, 4)
            pe.wait_ge(keys_in, 32)
            for h in range(PH):
                last = TR(banks(0, 2)[:, h * P:(h + 1) * P], keys_row[:, h, :], ident[:, :])
            last.then_inc(e_keys_ps, 1)
            pe.wait_ge(e_keys_made, 1)
            pe.wait_ge(e_consts, 1)

            def scores(wait, n, keys, par):
                wait(q_staged, n + 1)
                M(banks(4, 1)[:, 0:2 * PK], q_st[par][:, :], keys, start=True, stop=True).then_inc(s_ps, 1)

            def edge(parts, start, stop):
                for c in range(2):
                    last = M(banks(c, 1)[0:parts, :], zeros_bf[:, 0:parts], zmov_bf[:, :], start=start, stop=stop)
                return last

            def add_row(r, parts):
                for c in range(2):
                    last = M(banks(c, 1)[0:parts, :], diag[r][:, 0:parts], v_ring[r][:, c * 512:(c + 1) * 512],
                             start=False, stop=False)
                last.then_inc(v_free, 1)

            scores(pe.wait_ge, 0, keys_bd[:, 0, :], 0)
            with pe.Fori(0, NT) as t:
                reg(y_read, t + 1)
                edge(P, True, False)
                with pe.Fori(0, PH // 2) as hp:
                    for par in range(2):
                        n = t * PH + hp * 2 + par
                        scores(reg, n + 1, keys_bd[:, bass.ds(hp * 2 + (par + 1), 1), :].rearrange("p h n -> p (h n)"), 1 - par)
                        for k in range(TOPK):
                            reg(v_in[k % RING], n * 32 + 16 * (k // RING + 1))
                            reg(diag_made, n * TOPK + (k + 1))
                            add_row(k % RING, P)
                edge(P, False, True).then_inc(y_ps, 1)
            base = NT * PH * TOPK
            pe.wait_ge(y_read, NT + 1)
            edge(NS, True, False)
            for h in range(PH):
                if h + 1 < PH:
                    scores(pe.wait_ge, NT * PH + h + 1, keys_bd[:, h + 1, :], (h + 1) % 2)
                for k in range(4):
                    m = 4 * h + k
                    pe.wait_ge(v_in[m % RING], 16 * (NT * PH * 2 + m // RING + 1))
                    pe.wait_ge(diag_made, base + m + 1)
                    add_row(m % RING, NS)
            edge(NS, False, True).then_inc(y_ps, 1)


_INS = ['x_prompt', 'x_sample', 'cache_k', 'cache_v', 'state_conv', 'c_prompt', 'c_sample',
        'w_ada', 'b_ada', 'norm1_w', 'w_in', 'q_norm_w', 'k_norm_w', 'sinks', 'conv_w', 'conv_bias',
        'w_out', 'norm2_w', 'w_query', 'sub_keys', 'expert_u', 'expert_v']
_OUTS = [(1, NP, D), (NB, L, D), (1, 1, WIN, NKV, HD), (1, 1, WIN, NKV, HD), (1, 1, 2, D),
         (1, NB, WIN, NKV, HD), (1, NB, WIN, NKV, HD), (1, NB, 2, D)]


def kernel(**inputs):
    import numpy as _np
    import concourse.bacc as _bacc
    from concourse import mybir as _mybir
    from concourse.bass_utils import run_bass_kernel_spmd as _run

    nc = _bacc.Bacc("TRN2", target_bir_lowering=False, num_devices=1)
    arrays, args = {}, []
    for name in _INS:
        a = _np.ascontiguousarray(inputs[name])
        arrays[f"in_{name}_dram"] = a
        args.append(nc.dram_tensor(f"in_{name}_dram", a.shape, _mybir.dt.from_np(a.dtype), kind="ExternalInput").ap())
    for i, shape in enumerate(_OUTS):
        args.append(nc.dram_tensor(f"out_{i}_dram", shape, _mybir.dt.float32, kind="ExternalOutput").ap())
    build(nc, *args)
    r = _run(nc, [arrays], core_ids=[0])
    return tuple(r.results[0][f"out_{i}_dram"] for i in range(len(_OUTS)))
```

```python
from contextlib import ExitStack
from functools import partial

import concourse.bass as bass
from concourse import mybir

F32 = mybir.dt.float32
F32R = mybir.dt.float32r
I32 = mybir.dt.int32
U32 = mybir.dt.uint32
ALU = mybir.AluOpType
ACT = mybir.ActivationFunctionType
AX = mybir.AxisListType

P = 128
D = 1024
KC = D // P
NP = 1024
NT = NP // P
NB, L = 8, 4
NS = NB * L
T = NP + NS
NH, NKV, HD = 16, 4, 64
KVW = NKV * HD
QKV = D + 2 * KVW
NQK = NH + NKV
WIN = 128
EPS = 1e-6
SCALE = HD ** -0.5
NEG = -1e30
LOWEST = -3.0e38
PH, PK, TOPK = 8, 128, 16
NE = PK * PK
UNITS = NT * PH + 2
RING = 4
DIAGS = 8
IDXS = 4
V_SEED = DIAGS + TOPK
PER_UNIT = 16 * TOPK // RING
ABLK = 512
NBLK = 6 * D // ABLK
ARING = 3
ENGINES = 5
ARENA = 35060


def up32(at):
    return (at + 31) // 32 * 32


def build(nc, x_prompt, x_sample, cache_k, cache_v, state_conv, c_prompt, c_sample,
          w_ada, b_ada, norm1_w, w_in, q_norm_w, k_norm_w, sinks, conv_w, conv_bias,
          w_out, norm2_w, w_query, sub_keys, expert_u, expert_v,
          y_prompt, y_sample, new_k_prompt, new_v_prompt, new_conv_prompt,
          new_k_sample, new_v_sample, new_conv_sample):
    xp = x_prompt.rearrange("a (t p) d -> (a t) p d", p=P)
    xs = x_sample.rearrange("b l d -> (b l) d")
    yp = y_prompt.rearrange("a (t p) d -> (a t) p d", p=P)
    ys = y_sample.rearrange("b l d -> (b l) d")
    ck = cache_k.rearrange("a b w g d -> (a b) w (g d)")
    cv = cache_v.rearrange("a b w g d -> (a b) w (g d)")
    nks = new_k_sample.rearrange("a b w g d -> (a b) w (g d)")
    nvs = new_v_sample.rearrange("a b w g d -> (a b) w (g d)")
    w_ada_v = w_ada.rearrange("a (k p) n -> (a p) k n", p=P)
    w_in_v = w_in.rearrange("a (k p) n -> (a p) k n", p=P)
    w_out_v = w_out.rearrange("a (k p) n -> (a p) k n", p=P)
    w_query_v = w_query.rearrange("a (k p) n -> (a p) k n", p=P)
    keys_v = sub_keys.rearrange("a h c n d -> (a h) c n d")
    eu = expert_u.rearrange("a n d -> (a n) d")
    ev = expert_v.rearrange("a n d -> (a n) d")

    mod_p = nc.dram_tensor("mod_p", [1, 6 * D], F32, kind="Internal").ap()
    mod_s = nc.dram_tensor("mod_s", [NS, 6 * D], F32, kind="Internal").ap()
    x2_d = nc.dram_tensor("x2_d", [NT + 1, P, D], F32, kind="Internal").ap()
    h2_d = nc.dram_tensor("h2_d", [NT + 1, P, D], F32, kind="Internal").ap()

    q_dh = nc.dram_tensor("q_dh", [UNITS, P, P], F32, kind="Internal").ap()

    ctx = ExitStack()
    with ctx:
        def sb(name, shape, dt=F32):
            return ctx.enter_context(nc.sbuf_tensor(name, shape, dt))

        def sem(name):
            return ctx.enter_context(nc.semaphore(name))

        ident = sb("ident", [P, P])
        sel_s = sb("sel_s", [P, NS])
        eps = sb("eps", [P, 1])
        TOKENS_AT = up32(nc.sbuf_base)
        tokens_t = sb("tokens_t", [P, KC * (NT + 1) * P])
        hT = tokens_t[:, 0:KC * T].rearrange("p (k t) -> p k t", k=KC)
        oT = sb("oT", [P, KC, T])
        state_t = sb("state_t", [P, KC, NB * 2])
        new_t = sb("new_t", [P, KC, 2 + NB * 2])
        cw = sb("cw", [P, 4, KC])
        ARENA_AT = up32(nc.sbuf_base)
        arena = sb("arena", [P, ARENA])
        cursor = [0]

        def carve(*shape):
            n = 1
            for s in shape:
                n *= s
            v = arena[:, cursor[0]:cursor[0] + n]
            cursor[0] += n
            assert cursor[0] <= ARENA, cursor[0]
            if len(shape) == 2:
                v = v.rearrange("p (a b) -> p a b", a=shape[0])
            if len(shape) == 3:
                v = v.rearrange("p (a b c) -> p a b c", a=shape[0], b=shape[1])
            if len(shape) == 4:
                v = v.rearrange("p (a b c d) -> p a b c d", a=shape[0], b=shape[1], c=shape[2])
            return v

        def take(words):
            cursor[0] += words
            return cursor[0] - words

        def placed(name, at, *shape):
            return nc.alloc_sbuf_tensor_at(name, [P, *shape], F32R, offset=at)

        bank = ctx.enter_context(nc.psum_tensor("bank", [P, 8, 512], F32))

        def banks(a, n):
            return bank[:, a:a + n, :].rearrange("p a b -> p (a b)")

        passed = {e: sem(f"passed_{e}") for e in ("sp", "act", "dve", "pe", "pool")}
        stage_end = [sem(f"stage_end_{s}") for s in "ABSCD"]
        chain_dve, chain_act, chain_pool = sem("chain_dve"), sem("chain_act"), sem("chain_pool")

        def hold(eng, who, s, value):
            eng.wait_ge(s, value)
            eng.sem_inc(passed[who], 1)

        class Chain:
            def __init__(self, eng, s):
                self.eng, self.s, self.n = eng, s, 0

            def __call__(self, ins):
                self.n += 1
                ins.then_inc(self.s, 1)
                self.eng.wait_ge(self.s, self.n)

            def note(self, ins):
                self.n += 1
                ins.then_inc(self.s, 1)

            def settle(self):
                if self.n:
                    self.eng.wait_ge(self.s, self.n)

            def restart(self):
                self.settle()
                self.eng.sem_clear(self.s)
                self.n = 0

        def barrier(eng, s):
            eng.drain().then_inc(stage_end[s], 1)
            eng.wait_ge(stage_end[s], ENGINES)

        def scr(region, at, *shape):
            n = 1
            for s in shape:
                n *= s
            v = region[:, at:at + n]
            if len(shape) == 2:
                v = v.rearrange("p (a b) -> p a b", a=shape[0])
            return v, at + n

        w_qkv = carve(KC, QKV)
        mark_qkv = cursor[0]
        ada_w = [carve(KC, ABLK) for _ in range(ARING)]
        mod9 = carve(6 * D)
        bada9 = tokens_t[:, 0:6 * D]
        o_flat = oT[:, :, :].rearrange("p k t -> p (k t)")
        c9, at = scr(o_flat, 0, D)
        ec9, at = scr(o_flat, at, D)
        st16, at = scr(o_flat, at, D)
        cw4, at = scr(o_flat, at, D)
        cT, at = scr(o_flat, at, KC, NB + 1)

        cursor[0] = mark_qkv
        xt = [carve(D) for _ in range(2)]
        h_row = carve(D)
        A1, B1 = carve(D), carve(D)
        qkv = carve(QKV)
        sq = carve(NQK, HD)
        junk = sq[:, :, :].rearrange("p h d -> p (h d)")[:, 0:D]
        qk_w = carve(NQK, HD)
        smax = carve(4)
        nmax, sdif, esink, den, rden = (carve(2, 4) for _ in range(5))
        ssq, rms, rstd = carve(1), carve(1), carve(1)
        hss, hrms, hrs = carve(NQK), carve(NQK), carve(NQK)
        mark_attn = cursor[0]
        hT_now = carve(KC, P)
        kpad = carve(NKV, 2, 2, P)
        vpad = carve(2, NKV, 3 * HD)
        maskt = carve(3, 2, P)
        sink_row = carve(NH)
        qT_now = carve(KC, P)
        sm = [carve(4, 2 * P) for _ in range(2)]
        pe_ = [carve(4, 2 * P) for _ in range(2)]
        pT = carve(2, 4, P)
        cursor[0] = mark_attn
        ck_sb, cv_sb = carve(NB, KVW), carve(NB, KVW)
        kcT = carve(NKV, NB * WIN + NS)
        s_mask = carve(NB * WIN + NS)
        qz = xt[1][:, 0:NKV * P].rearrange("p (g r e t) -> p g r e t", g=NKV, r=2, e=2)
        sink_col = carve(NKV)
        cursor[0] = 0
        s_sm, s_pT = carve(NB * WIN + NS), carve(NB + 1, P)
        cursor[0] = 0
        w_c = [carve(KC, P) for _ in range(5)]
        w_hi = [placed(f"w_hi_{r}", ARENA_AT + 4 * take(D), KC, P) for r in range(2)]
        w_lo = [placed(f"w_lo_{r}", ARENA_AT + 4 * take(D), KC, P) for r in range(2)]
        hT_hi = placed("hT_hi", ARENA_AT + 4 * take(KC * T), KC, T)
        hT_lo = placed("hT_lo", TOKENS_AT, KC, T)
        cu_p = carve(2 + NP)
        cu_s = carve(NB, 2 + L)
        cw_now = carve(4)
        c_end = cursor[0]
        cursor[0] = 0
        u_ring = [carve(D) for _ in range(RING)]
        v_ring = [carve(D) for _ in range(RING)]
        h2_next, h2_now, x2_now, y_now, prod = carve(D), carve(D), carve(D), carve(D), carve(2, D)
        G2 = carve(D)
        diag = [carve(P) for _ in range(DIAGS)]
        keys_bd = carve(PH + 1, 2 * PK)
        keys_row = y_now[:, :].rearrange("p (h c) -> p h c", h=PH)
        q_st = [carve(P) for _ in range(2)]
        s_sb = [carve(2, PK) for _ in range(2)]
        cand, cand_cut = carve(TOPK, TOPK), carve(TOPK, TOPK)
        onehot, s_cut = cand_cut, cand_cut[:, 0:PK // TOPK, :].rearrange("p a b -> p (a b)")
        top_v, top_f = carve(2, TOPK), carve(2, TOPK)
        top_i = carve(2, TOPK).bitcast(U32)
        best_v, best_f = carve(TOPK), carve(TOPK)
        best_i, part_i = carve(TOPK).bitcast(U32), carve(TOPK).bitcast(U32)
        i_half = carve(2, TOPK)
        iota16 = carve(TOPK)
        idx = [carve(TOPK).bitcast(I32) for _ in range(IDXS)]
        gate_e, gsum, nbest = carve(TOPK), carve(1), carve(1)
        gate, dot, act_dot, wgt = ([carve(TOPK) for _ in range(2)] for _ in range(4))
        zeros_bf = carve(P // 2).bitcast(mybir.dt.bfloat16)
        zmov_bf = carve(256).bitcast(mybir.dt.bfloat16)
        ssq2, rms2, rstd2 = carve(1), carve(1), carve(1)
        cursor[0] = max(cursor[0], c_end)
        wo_sb = carve(KC, D)
        d_rows_at = cursor[0]
        u_sb, y_c, sg_c, sg_a, mg = (carve(T) for _ in range(5))
        cursor[0] = d_rows_at
        G1, A2, B2 = carve(D), carve(D), carve(D)
        xd, h2 = carve(D), carve(D)
        mT = carve(KC, P)
        wq_sb, at = scr(tokens_t, 0, KC, D)
        q_out, at = scr(tokens_t, at, PH, P)
        n2 = q_out[:, :, :].rearrange("p h t -> p (h t)")
        new_row = prod[:, 0, :]

        consts_made, small_in, qkv_w_in, keys_in = sem("consts_made"), sem("small_in"), sem("qkv_w_in"), sem("keys_in")
        ada_in = [sem(f"ada_in_{r}") for r in range(ARING)]
        exp_c, silu_made, small_ps, small_made = sem("exp_c"), sem("silu_made"), sem("small_in_psum"), sem("small_made")
        ada_free, ada_ps, mod_stored = sem("ada_free"), sem("ada_in_psum"), sem("mod_stored")
        rows_in, scale1_made, attn_zeroed = sem("rows_in"), sem("scale1_made"), sem("attn_zeroed")
        x_in = [sem(f"x_in_{u}") for u in range(2)]
        x_free, rms_made, h_made, hT_ps, hT_copied, hT_kept = (sem(n) for n in (
            "x_free", "rms_made", "h_made", "hT_in_psum", "hT_copied", "hT_kept"))
        qkv_ps, qkv_out, qkv_free, hss_made, hrms_made, qk_normed, v_placed = (sem(n) for n in (
            "qkv_in_psum", "qkv_out", "qkv_free", "head_sums", "head_rms", "qk_normed", "v_placed"))
        qkT_ps, qT_made, kpad_made, score_ps, score_read, max_made, exp_made, den_made, p_made = (sem(n) for n in (
            "qkT_in_psum", "qT_made", "kpad_made", "scores_in_psum", "scores_read", "max_made", "exp_made",
            "den_made", "p_made"))
        pT_ps, pT0_made, pT1_made, pv_ps, o_kept, kv_stored = (sem(n) for n in (
            "pT_in_psum", "pT0_made", "pT1_made", "pv_in_psum", "o_kept", "kv_stored"))
        srow_in = sem("s_modulation_in")
        sx_in, scache_in, s_rows, s_act, s_dve, s_pe, s_stored = (sem(n) for n in (
            "s_x_in", "s_cache_in", "s_rows", "s_act_step", "s_dve_step", "s_pe_step", "s_stored"))
        s_kc0, s_kc1, s_kcps, mask_s_made = sem("s_kc0"), sem("s_kc1"), sem("s_kc_in_psum"), sem("mask_s_made")
        wc_in = [sem(f"wc_in_{r}") for r in range(5)]
        hi_made, lo_made, w_hi_made, w_split = sem("hi_made"), sem("lo_made"), sem("w_hi_made"), sem("w_split")
        conv_ps, conv_read, u_made, gate_c_made, gate_a_made, cu_made = (sem(n) for n in (
            "conv_in_psum", "conv_read", "u_made", "gate_c_made", "gate_a_made", "cu_made"))
        wo_in, wq_in, d_rows, new_ps, new_made, new_stored = (sem(n) for n in (
            "w_out_in", "w_query_in", "d_rows_in", "new_conv_in_psum", "new_conv_made", "new_conv_stored"))
        xd_in = sem("xd_in")
        mT_made, q_stored, out_ps, x2_made, rms2_made, h2_made, h2T_ps, h2T_made, qry_ps, qry_kept = (
            sem(n) for n in ("mT_made", "queries_stored", "out_in_psum", "x2_made", "rms2_made", "h2_made",
                             "h2T_in_psum", "h2T_made", "query_in_psum", "query_kept"))
        x2h2_stored = sem("x2h2_stored")
        e_consts, e_keys_ps, e_keys_made, e_g2_in = (sem(n) for n in (
            "e_consts", "keys_in_psum", "keys_made", "g2_in"))
        u_in = [sem(f"u_in_{r}") for r in range(RING)]
        v_in = [sem(f"v_in_{r}") for r in range(RING)]
        q_in = [sem(f"q_in_{r}") for r in range(2)]
        u_free, v_free, s_ps, s_out, best_made, gate_exp, idx_made, gelu_made, wgt_made, diag_made = (
            sem(n) for n in ("u_free", "v_free", "s_in_psum", "s_out", "best_made", "gate_exp",
                             "idx_made", "gelu_made", "wgt_made", "diag_made"))
        y_ps, y_read, y_made, y_stored, y_free, h2_in, h2_taken, x2_in = (sem(n) for n in (
            "y_in_psum", "y_read", "y_made", "y_stored", "y_free", "h2_in", "h2_taken", "x2_in"))

        block = ctx.enter_context(nc.Block())

        C_U, C_POST, C_PRE, C_GA, C_GC = QKV, QKV + D, QKV + 2 * D, QKV + 3 * D, QKV + 4 * D
        C_KINDS = [C_U, C_PRE, C_POST, C_GC, C_GA]

        @block.sync
        def _(sp):
            sp.dma_start(c9[0:NB, :], c_sample).then_inc(small_in, 16)
            sp.dma_start(c9[NB:NB + 1, :], c_prompt).then_inc(small_in, 16)
            sp.dma_start(st16[0:NB * 2, :], state_conv.rearrange("a b r d -> (a b r) d")).then_inc(small_in, 16)
            sp.dma_start(cw4[0:3, :], conv_w.rearrange("a r d -> (a r) d")).then_inc(small_in, 16)
            sp.dma_start(cw4[3:4, :], conv_bias).then_inc(small_in, 16)
            sp.dma_start(bada9[0:NB + 1, :], b_ada.to_broadcast([NB + 1, 6 * D])).then_inc(small_in, 16)
            with sp.Fori(0, NBLK // ARING) as j:
                for r in range(ARING):
                    hold(sp, "sp", ada_free, j * ARING + r + 1)
                    sp.dma_start(ada_w[r][:, :, :], w_ada_v[:, :, bass.ds(j * (ARING * ABLK) + r * ABLK, ABLK)]
                                 ).then_inc(ada_in[r], 16)
            sp.dma_start(w_qkv[:, :, :], w_in_v[:, :, 0:QKV]).then_inc(qkv_w_in, 16)
            barrier(sp, 0)
            sp.dma_start(A1[:, :], mod_p[:, D:2 * D].to_broadcast([P, D])).then_inc(rows_in, 16)
            sp.dma_start(B1[:, :], mod_p[:, 0:D].to_broadcast([P, D])).then_inc(rows_in, 16)
            sp.dma_start(junk[:, :], norm1_w.to_broadcast([P, D])).then_inc(rows_in, 16)
            sp.dma_start(qk_w[:, 0, :], q_norm_w.to_broadcast([P, HD])).then_inc(rows_in, 16)
            sp.dma_start(qk_w[:, NH, :], k_norm_w.to_broadcast([P, HD])).then_inc(rows_in, 16)
            sp.dma_start(sink_row[:, :], sinks.to_broadcast([P, NH])).then_inc(rows_in, 16)
            with sp.Fori(0, NT // 2) as i:
                for u in range(2):
                    hold(sp, "sp", x_free, i * 2 + u + 1)
                    sp.dma_start(xt[u][:, :], xp[bass.ds(i * 2 + u, 1), :, :].rearrange("a p d -> (a p) d")
                                 ).then_inc(x_in[u], 16)
            sp.wait_ge(qk_normed, NT)
            sp.dma_start(new_k_prompt.rearrange("a b w g d -> (a b w) (g d)"), qkv[:, D:D + KVW]).then_inc(kv_stored, 16)
            sp.dma_start(new_v_prompt.rearrange("a b w g d -> (a b w) (g d)"), qkv[:, D + KVW:QKV]).then_inc(kv_stored, 16)
            sp.wait_ge(kv_stored, 32)
            barrier(sp, 1)
            sp.dma_start(xt[0][0:NS, :], xs).then_inc(sx_in, 16)
            sp.dma_start(A1[0:NS, :], mod_s[:, D:2 * D]).then_inc(srow_in, 16)
            sp.dma_start(B1[0:NS, :], mod_s[:, 0:D]).then_inc(srow_in, 16)
            sp.dma_start(h_row[0:NS, :], norm1_w.to_broadcast([NS, D])).then_inc(srow_in, 16)
            sp.dma_start(ck_sb[:, :, :], ck.rearrange("b w c -> w b c")).then_inc(scache_in, 16)
            sp.dma_start(cv_sb[:, :, :], cv.rearrange("b w c -> w b c")).then_inc(scache_in, 16)
            with nc.allow_non_contiguous_dma(reason="one sink for each quadrant of rows and group"):
                for q in range(4):
                    sp.dma_start(sink_col[32 * q:32 * q + 32, :],
                                 sinks.rearrange("a (g q) -> a g q", q=4)[:, :, q].to_broadcast([32, NKV])).then_inc(s_rows, 16)
            sp.dma_start(nks[:, 0:WIN - L, :], ck[:, L:WIN, :]).then_inc(s_stored, 16)
            sp.dma_start(nvs[:, 0:WIN - L, :], cv[:, L:WIN, :]).then_inc(s_stored, 16)
            sp.wait_ge(s_dve, 3)
            for b in range(NB):
                sp.dma_start(nks[b, WIN - L:WIN, :], qkv[L * b:L * b + L, D:D + KVW]).then_inc(s_stored, 16)
                sp.dma_start(nvs[b, WIN - L:WIN, :], qkv[L * b:L * b + L, D + KVW:QKV]).then_inc(s_stored, 16)
            sp.wait_ge(s_stored, 16 * (2 + 2 * NB))
            barrier(sp, 2)
            with sp.Fori(0, KC // 2) as i:
                for n in range(10):
                    hold(sp, "sp", w_split, i * 10 + n + 1)
                    sp.dma_start(w_c[n % 5][:, :, :],
                                 w_in_v[:, :, bass.ds(i * (2 * P) + (C_KINDS[n % 5] + (n // 5) * P), P)]
                                 ).then_inc(wc_in[n % 5], 16)
            sp.dma_start(wo_sb[:, :, :], w_out_v).then_inc(wo_in, 16)
            barrier(sp, 3)
            sp.dma_start(n2[:, :], norm2_w.to_broadcast([P, D])).then_inc(d_rows, 16)
            sp.dma_start(G1[:, :], mod_p[:, 2 * D:3 * D].to_broadcast([P, D])).then_inc(d_rows, 16)
            sp.dma_start(A2[:, :], mod_p[:, 4 * D:5 * D].to_broadcast([P, D])).then_inc(d_rows, 16)
            sp.dma_start(B2[:, :], mod_p[:, 3 * D:4 * D].to_broadcast([P, D])).then_inc(d_rows, 16)
            sp.dma_start(xd[:, :], xp[0, :, :]).then_inc(xd_in, 16)
            sp.dma_start(wq_sb[:, :, :], w_query_v).then_inc(wq_in, 16)
            sp.dma_start(keys_row[:, :, 0:HD], keys_v[:, 0, :, :].rearrange("h n d -> n h d")).then_inc(keys_in, 16)
            sp.dma_start(keys_row[:, :, HD:P], keys_v[:, 1, :, :].rearrange("h n d -> n h d")).then_inc(keys_in, 16)
            sp.dma_start(G2[:, :], mod_p[:, 5 * D:6 * D].to_broadcast([P, D])).then_inc(e_g2_in, 16)
            barrier(sp, 4)
            sp.dma_start(h2_next[:, :], h2_d[0, :, :]).then_inc(h2_in, 16)
            sp.dma_start(x2_now[:, :], x2_d[0, :, :]).then_inc(x2_in, 16)
            sp.sem_inc(y_free, 1)
            with sp.Fori(0, NT - 1) as t:
                sp.dma_start(xd[:, :], xp[bass.ds(t + 1, 1), :, :].rearrange("a p d -> (a p) d")).then_inc(xd_in, 16)
                hold(sp, "sp", h2_taken, t + 1)
                hold(sp, "sp", x2h2_stored, t * 32 + 64)
                sp.dma_start(h2_next[:, :], h2_d[bass.ds(t + 1, 1), :, :].rearrange("a p d -> (a p) d")).then_inc(h2_in, 16)
                hold(sp, "sp", y_made, t + 1)
                sp.dma_start(yp[bass.ds(t, 1), :, :].rearrange("a p d -> (a p) d"), y_now[:, :]).then_inc(y_stored, 16)
                sp.dma_start(x2_now[:, :], x2_d[bass.ds(t + 1, 1), :, :].rearrange("a p d -> (a p) d")).then_inc(x2_in, 16)
                hold(sp, "sp", y_stored, t * 16 + 16)
                sp.sem_inc(y_free, 1)
            sp.dma_start(G1[0:NS, :], mod_s[:, 2 * D:3 * D]).then_inc(d_rows, 16)
            sp.dma_start(A2[0:NS, :], mod_s[:, 4 * D:5 * D]).then_inc(d_rows, 16)
            sp.dma_start(B2[0:NS, :], mod_s[:, 3 * D:4 * D]).then_inc(d_rows, 16)
            sp.dma_start(xd[0:NS, :], xs).then_inc(xd_in, 16)
            sp.wait_ge(q_stored, 16 * NT)
            sp.dma_start(n2[0:NS, :], norm2_w.to_broadcast([NS, D])).then_inc(d_rows, 16)
            sp.wait_ge(h2_taken, NT)
            sp.wait_ge(x2h2_stored, 32 * (NT + 1))
            for q in range(4):
                sp.dma_start(h2_next[NS * q:NS * q + NS, :], h2_d[NT, 0:NS, :]).then_inc(h2_in, 16)
            sp.wait_ge(y_made, NT)
            sp.dma_start(yp[NT - 1, :, :], y_now[:, :]).then_inc(y_stored, 16)
            sp.dma_start(x2_now[0:NS, :], x2_d[NT, 0:NS, :]).then_inc(x2_in, 16)
            sp.dma_start(G2[0:NS, :], mod_s[:, 5 * D:6 * D]).then_inc(e_g2_in, 16)
            sp.wait_ge(y_stored, 16 * NT)
            sp.sem_inc(y_free, 1)
            sp.wait_ge(y_made, NT + 1)
            sp.dma_start(ys, y_now[0:NS, :]).then_inc(y_stored, 16)
            sp.wait_ge(y_stored, 16 * (NT + 1))

        @block.gpsimd
        def _(pool):
            link = Chain(pool, chain_pool)

            def where(view, pattern, base, mult, cmp, fill):
                link(pool.affine_select(out=view, in_=view, compare_op=cmp, fill=fill, base=base,
                                        pattern=pattern, channel_multiplier=mult))

            link(pool.memset(ident[:, :], 0.0))
            where(ident[:, :], [[-1, P]], 0, 1, ALU.not_equal, 1.0)
            link(pool.memset(sel_s[:, :], 0.0))
            for q in range(4):
                where(sel_s[:, :], [[-1, NS]], -NS * q, 1, ALU.not_equal, 1.0)
            link(pool.memset(eps[:, :], EPS))
            pool.sem_inc(consts_made, 1)
            barrier(pool, 0)
            link(pool.memset(maskt[:, :, :, :], 0.0))
            for m, own in ((0, 0), (1, 1), (2, 0)):
                where(maskt[:, m, own, :], [[-1, P]], 0, 1, ALU.is_ge, NEG)
                if m:
                    where(maskt[:, m, 1 - own, :], [[1, P]], -1, -1, ALU.is_ge, NEG)
            link(pool.memset(maskt[:, 0, 1, :], NEG))
            link(pool.memset(kpad[:, :, :, :, :], 0.0))
            link(pool.memset(vpad[:, :, :, :], 0.0))
            pool.sem_inc(attn_zeroed, 1)
            link.restart()
            with pool.Fori(0, NT // 2) as i:
                for u in range(2):
                    t = i * 2 + u
                    hold(pool, "pool", hT_copied, t + 1)
                    link(pool.tensor_copy(hT[:, :, bass.ds(t * P, P)], hT_now[:, :, :]))
                    pool.sem_inc(hT_kept, 1)
                    hold(pool, "pool", qkv_out, t + 1)
                    hold(pool, "pool", pv_ps, t * 4 + 4)
                    for half in range(2):
                        link(pool.tensor_copy(vpad[:, u, :, 2 * HD * half:2 * HD * half + HD],
                                              qkv[:, D + KVW:QKV].rearrange("p (g d) -> p g d", g=NKV)))
                    pool.sem_inc(v_placed, 1)
                link.restart()
            barrier(pool, 1)
            link(pool.memset(s_mask[:, :], 0.0))
            link(pool.memset(qz[:, :, :, :, :], 0.0))
            cache = s_mask[0:NS, 0:NB * WIN].rearrange("p (b j) -> p b j", b=NB)
            new = s_mask[0:NS, NB * WIN:].rearrange("p (b l) -> p b l", b=NB)
            where(cache, [[-L, NB], [0, WIN]], 0, 1, ALU.is_ge, NEG)
            where(cache, [[L, NB], [0, WIN]], L - 1, -1, ALU.is_ge, NEG)
            where(cache, [[L, NB], [1, WIN]], -1, -1, ALU.is_ge, NEG)
            where(new, [[-L, NB], [0, L]], 0, 1, ALU.is_ge, NEG)
            where(new, [[L, NB], [0, L]], L - 1, -1, ALU.is_ge, NEG)
            where(new, [[-L, NB], [-1, L]], 0, 1, ALU.is_ge, NEG)
            pool.sem_inc(mask_s_made, 1)
            barrier(pool, 2)
            barrier(pool, 3)
            link(pool.iota(part_i, pattern=[[1, TOPK]], base=0, channel_multiplier=0))
            link(pool.tensor_copy(iota16, part_i))
            link(pool.memset(keys_bd[:, :, :], 0.0))
            link(pool.memset(zeros_bf, 0.0))
            link(pool.memset(zmov_bf, 0.0))
            pool.sem_inc(e_consts, 1)
            barrier(pool, 4)
            def gather_u(n, k, buf):
                hold(pool, "pool", u_free, n * TOPK + (k + 1))
                pool.indirect_dma_start(out=u_ring[k % RING][:, :], out_offset=None, in_=eu,
                                        in_offset=bass.IndirectOffsetOnAxis(ap=idx[buf][:, k:k + 1], axis=0)
                                        ).then_inc(u_in[k % RING], 16)

            def gather_v(n, k, buf):
                hold(pool, "pool", v_free, n * TOPK + (V_SEED + k + 1 - RING))
                pool.indirect_dma_start(out=v_ring[k % RING][:, :], out_offset=None, in_=ev,
                                        in_offset=bass.IndirectOffsetOnAxis(ap=idx[buf][:, k:k + 1], axis=0)
                                        ).then_inc(v_in[k % RING], 16)

            def pool_period(n, u):
                hold(pool, "pool", idx_made, n + 1)
                for k in range(TOPK):
                    gather_u(n, k, u % IDXS)
                    gather_v(n - 1, k, (u - 1) % IDXS)

            hold(pool, "pool", idx_made, 1)
            for k in range(TOPK):
                gather_u(0, k, 0)
            with pool.Fori(0, NT - 1) as t:
                for u in range(1, PH + 1):
                    pool_period(t * PH + u, u)
            for n in range((NT - 1) * PH + 1, UNITS):
                pool_period(n, n)
            for k in range(TOPK):
                gather_v(UNITS - 1, k, (UNITS - 1) % IDXS)

        @block.scalar
        def _(act):
            link = Chain(act, chain_act)
            act.wait_ge(small_in, 16 * 6)
            nc.scalar.activation(ec9[0:NB + 1, :], c9[0:NB + 1, :], ACT.Exp, scale=-1.0).then_inc(exp_c, 1)
            act.wait_ge(ada_free, NBLK + ARING)
            act.dma_start(mod_p, mod9[NB:NB + 1, :]).then_inc(mod_stored, 16)
            for l in range(L):
                act.dma_start(mod_s.rearrange("(b l) n -> l b n", l=L)[l], mod9[0:NB, :]).then_inc(mod_stored, 16)
            act.wait_ge(mod_stored, 16 * (1 + L))
            barrier(act, 0)

            def token_rms(x, out_sq, s, r, parts):
                link(nc.scalar.activation(out_sq[0:parts, :], x[0:parts, :], ACT.Square, accum_out=s[0:parts, :]))
                return nc.scalar.activation(r[0:parts, :], s[0:parts, :], ACT.Sqrt, scale=1.0 / D, bias=eps[0:parts, :])

            act.wait_ge(scale1_made, 1)

            def row_rms(wait, n, u, count):
                wait(x_in[u], count)
                link(token_rms(xt[u], junk, ssq, rms, P))
                act.sem_inc(rms_made, 1)

            def copy_hT(wait, n):
                wait(hT_ps, n + 1)
                wait(hT_kept, n + 1)
                link(nc.scalar.copy(hT_now[:, :, :].rearrange("p k t -> p (k t)"), banks(0, 2)))
                act.sem_inc(hT_copied, 1)

            def copy_qkv(wait, n):
                wait(qkv_ps, n * 3 + 3)
                wait(v_placed, n + 1)
                link(nc.scalar.copy(qkv[:, :], banks(0, 3)))
                act.sem_inc(qkv_out, 1)
                link(nc.scalar.activation(sq[:, :, :].rearrange("p h d -> p (h d)"), qkv[:, 0:D + KVW], ACT.Square))
                act.sem_inc(hss_made, 1)

            def head_rms(wait, n):
                wait(hss_made, n * 2 + 2)
                link(nc.scalar.activation(hrms[:, :], hss[:, :], ACT.Sqrt, scale=1.0 / HD, bias=eps[:, :]))
                act.sem_inc(hrms_made, 1)

            def copy_qT(wait, n):
                wait(qkT_ps, n + 1)
                link(nc.scalar.copy(qT_now[:, :, :].rearrange("p k t -> p (k t)"), banks(0, 2)))
                act.sem_inc(qT_made, 1)

            def exps(wait, t, g):
                wait(max_made, t * 4 + (g + 1))
                b = g % 2
                for h in range(4):
                    link.note(nc.scalar.activation(pe_[b][:, h, :], sm[b][:, h, :], ACT.Exp, bias=nmax[:, b, h:h + 1],
                                                   accum_out=den[:, b, h:h + 1]))
                link(nc.scalar.activation(esink[:, b, :], sdif[:, b, :], ACT.Exp))
                act.sem_inc(exp_made, 1)

            def normalise(wait, t, g):
                wait(den_made, t * 4 + (g + 1))
                b = g % 2
                for h in range(4):
                    link.note(nc.scalar.activation(pe_[b][:, h, :], pe_[b][:, h, :], ACT.Copy, scale=rden[:, b, h:h + 1]))
                link.settle()
                act.sem_inc(p_made, 1)

            def copy_pT(wait, t, g):
                wait(pT_ps, t * 4 + (g + 1))
                wait(pv_ps, t * 4 + (g + 4))
                link(nc.scalar.copy(pT[:, 0, :, :].rearrange("p h t -> p (h t)"), banks(5, 1)))
                act.sem_inc(pT0_made, 1)

            def act_tile(wait, t, u, x_count, more, more2):
                if more:
                    copy_hT(wait, t + 1)
                exps(wait, t, 0)
                exps(wait, t, 1)
                normalise(wait, t, 0)
                copy_pT(wait, t, 0)
                exps(wait, t, 2)
                normalise(wait, t, 1)
                copy_pT(wait, t, 1)
                if more:
                    copy_qkv(wait, t + 1)
                exps(wait, t, 3)
                normalise(wait, t, 2)
                if more:
                    head_rms(wait, t + 1)
                copy_pT(wait, t, 2)
                normalise(wait, t, 3)
                if more:
                    copy_qT(wait, t + 1)
                copy_pT(wait, t, 3)
                if more2:
                    row_rms(wait, t + 2, u, x_count)

            def reg(s, v):
                hold(act, "act", s, v)

            w = act.wait_ge
            row_rms(w, 0, 0, 16)
            copy_hT(w, 0)
            row_rms(w, 1, 1, 16)
            copy_qkv(w, 0)
            head_rms(w, 0)
            copy_qT(w, 0)
            link.restart()
            with act.Fori(0, NT // 2 - 1) as i:
                for u in range(2):
                    act_tile(reg, i * 2 + u, u, i * 16 + 32, True, True)
                link.restart()
            act_tile(w, NT - 2, 0, None, True, False)
            act_tile(w, NT - 1, 1, None, False, False)
            barrier(act, 1)
            act.wait_ge(sx_in, 16)
            link(token_rms(xt[0], junk, ssq, rms, NS))
            act.sem_inc(s_act, 1)
            act.wait_ge(s_pe, 1)
            link(nc.scalar.copy(hT[:, :, NP:T], banks(0, 1)[:, 0:KC * NS].rearrange("p (k t) -> p k t", k=KC)))
            act.sem_inc(s_act, 1)
            act.wait_ge(s_kcps, 1)
            for e in range(2):
                for half in range(2):
                    link.note(nc.scalar.copy(kcT[HD * half:HD * half + HD, e, 0:NB * WIN],
                                             banks(3, 2)[HD * e:HD * e + HD, :]))
            link.settle()
            act.sem_inc(s_kc0, 1)
            act.wait_ge(s_pe, 2)
            link(nc.scalar.copy(qkv[0:NS, :], banks(0, 3)[0:NS, :]))
            act.sem_inc(s_act, 1)
            link(nc.scalar.activation(sq[0:NS, :, :].rearrange("p h d -> p (h d)"), qkv[0:NS, 0:D + KVW], ACT.Square))
            act.sem_inc(s_act, 1)
            act.wait_ge(s_dve, 2)
            link(nc.scalar.activation(hrms[0:NS, :], hss[0:NS, :], ACT.Sqrt, scale=1.0 / HD, bias=eps[0:NS, :]))
            act.sem_inc(s_act, 1)
            for g in range(NKV):
                act.wait_ge(s_dve, 5 + 4 * g)
                link(nc.scalar.activation(s_sm[:, :], s_sm[:, :], ACT.Exp, bias=nmax[:, 0, 0:1], accum_out=den[:, 0, 0:1]))
                link(nc.scalar.activation(esink[:, 0, 0:1], sdif[:, 0, 0:1], ACT.Exp))
                act.sem_inc(s_act, 1)
                act.wait_ge(s_dve, 6 + 4 * g)
                link(nc.scalar.activation(s_sm[:, :], s_sm[:, :], ACT.Copy, scale=rden[:, 0, 0:1]))
                act.sem_inc(s_act, 1)
            barrier(act, 2)
            link.restart()
            for k in range(KC):
                nc.scalar.copy(hT_hi[:, k, :], hT[:, k, :]).then_inc(hi_made, 1)

            def split_hi(i, n):
                hold(act, "act", wc_in[n % 5], i * 32 + 16 * (n // 5 + 1))
                hold(act, "act", conv_ps, i * 10 + (n + 4))
                nc.scalar.copy(w_hi[n % 2][:, :, :], w_c[n % 5][:, :, :]).then_inc(w_hi_made, 1)

            def act_pair(i, last):
                for j in range(2):
                    b_u, b_gc, b_ga = (3 * ((5 * j + n) % 2) for n in (0, 3, 4))
                    split_hi(i, 5 * j + 1)
                    hold(act, "act", conv_ps, i * 10 + (5 * j + 6))
                    hold(act, "act", cu_made, i * 2 + (j + 1))
                    link(nc.scalar.copy(u_sb[:, :], banks(b_u, 3)[:, 0:T]))
                    act.sem_inc(conv_read, 1)
                    act.sem_inc(u_made, 1)
                    for n in (2, 3, 4):
                        split_hi(i, 5 * j + n)
                    hold(act, "act", conv_ps, i * 10 + (5 * j + 9))
                    hold(act, "act", conv_read, i * 10 + (5 * j + 5))
                    link(nc.scalar.activation(sg_c[:, :], banks(b_gc, 3)[:, 0:T], ACT.Sigmoid))
                    act.sem_inc(conv_read, 1)
                    act.sem_inc(gate_c_made, 1)
                    if not (last and j == 1):
                        split_hi(i, 5 * j + 5)
                    hold(act, "act", conv_ps, i * 10 + (5 * j + 10))
                    link(nc.scalar.activation(sg_a[:, :], banks(b_ga, 3)[:, 0:T], ACT.Sigmoid))
                    act.sem_inc(conv_read, 1)
                    act.sem_inc(gate_a_made, 1)

            split_hi(0, 0)
            with act.Fori(0, KC // 2 - 1) as i:
                act_pair(i, False)
                link.restart()
            act_pair(KC // 2 - 1, True)
            link.restart()
            barrier(act, 3)
            act.wait_ge(new_ps, 1)
            link(nc.scalar.copy(new_row[0:2 + NB * 2, :], banks(0, 2)[0:2 + NB * 2, :]))
            act.dma_start(new_conv_prompt.rearrange("a b r d -> (a b r) d"), new_row[0:2, :]).then_inc(new_stored, 16)
            act.dma_start(new_conv_sample.rearrange("a b r d -> (a b r) d"), new_row[2:2 + NB * 2, :]).then_inc(new_stored, 16)
            act.sem_inc(new_made, 1)

            def d_rms(wait, t, x, h, x_at, parts):
                wait(x2_made, t + 1)
                link(token_rms(x, h, ssq2, rms2, parts))
                act.sem_inc(rms2_made, 1)
                act.dma_start(x_at, x[0:parts, :]).then_inc(x2h2_stored, 16)

            def d_store_h2(wait, t, h, h_at, parts):
                wait(h2_made, t + 1)
                act.dma_start(h_at, h[0:parts, :]).then_inc(x2h2_stored, 16)

            def d_keep_h2T(wait, t, hT_, b, parts):
                wait(h2T_ps, t + 1)
                link(nc.scalar.copy(hT_[:, :, 0:parts], banks(b, 2).rearrange("p (k t) -> p k t", k=KC)[:, :, 0:parts]))
                act.sem_inc(h2T_made, 1)

            def d_store_queries(wait, t, b, q_at):
                wait(qry_ps, t + 1)
                link(nc.scalar.copy(q_out[:, :, :], banks(b, 2).rearrange("p (h t) -> p h t", h=PH)))
                act.sem_inc(qry_kept, 1)
                act.dma_start(q_at, q_out[:, :, :]).then_inc(q_stored, 16)

            def d_store_sample_queries():
                act.wait_ge(qry_ps, NT + 1)
                link(nc.scalar.copy(q_out[:, 0:2, :].rearrange("p j (q t) -> p (j q) t", q=4),
                                    banks(2, 2).rearrange("p (h t) -> p h t", h=PH)[:, :, 0:NS]))
                act.dma_start(q_dh[NT * PH:UNITS, :, :].rearrange("h p t -> p h t"), q_out[:, 0:2, :]).then_inc(q_stored, 16)

            w = act.wait_ge
            d_rms(w, 0, xd, h2, x2_d[0, :, :], P)
            d_store_h2(w, 0, h2, h2_d[0, :, :], P)
            d_keep_h2T(w, 0, mT, 6, P)
            d_store_queries(w, 0, 2, q_dh[0:PH, :, :].rearrange("h p t -> p h t"))
            w(q_stored, 16)
            w(x2h2_stored, 32)
            w(new_stored, 32)
            barrier(act, 4)
            link.restart()

            def load_query(q_at, par):
                act.dma_start(q_st[par][:, :], q_at).then_inc(q_in[par], 16)

            def keep_scores(n, par, sample=False):
                reg(s_ps, n + 1)
                if sample:
                    for q in range(4):
                        link.note(nc.scalar.copy(s_sb[par][NS * q:NS * q + NS, :, :].rearrange("p c n -> p (c n)"),
                                                 banks(5, 2)[NS * q:NS * q + NS, 2 * PK * q:2 * PK * q + 2 * PK]))
                    link.settle()
                else:
                    link(nc.scalar.copy(s_sb[par][:, :, :].rearrange("p c n -> p (c n)"), banks(4, 1)[:, 0:2 * PK]))
                act.sem_inc(s_out, 1)

            def gate_exps(n):
                reg(best_made, n + 1)
                link(nc.scalar.activation(gate_e[:, :], best_v[:, :], ACT.Exp, bias=nbest[:, :], accum_out=gsum[:, :]))
                act.sem_inc(gate_exp, 1)

            def activate_dots(n, par):
                reg(u_free, n * TOPK + (RING + TOPK))
                link(nc.scalar.activation(act_dot[par][:, :], dot[par][:, :], ACT.Gelu))
                act.sem_inc(gelu_made, 1)

            def make_diag(n, par, k, parts):
                reg(v_free, n * TOPK + (V_SEED + k + 1 - DIAGS))
                base = ident if parts == P else sel_s
                nc.scalar.activation(diag[k % DIAGS][:, 0:parts], base[:, :], ACT.Copy, scale=wgt[par][:, k:k + 1]
                                     ).then_inc(diag_made, 1)

            load_query(q_dh[0, :, :], 0)
            load_query(q_dh[1, :, :], 1)
            keep_scores(0, 0)
            load_query(q_dh[2, :, :], 0)
            gate_exps(0)
            keep_scores(1, 1)
            gate_exps(1)
            link.restart()

            def act_period(n, u, after8=None, load=None, parts=P, picks="prompt"):
                activate_dots(n - 1, (u - 1) % 2)
                if load is not None:
                    reg(s_ps, n + 1)
                    load_query(load, u % 2)
                reg(wgt_made, n)
                for k in range(TOPK):
                    make_diag(n - 1, (u - 1) % 2, k, parts)
                    if k == 3 and picks is not None:
                        keep_scores(n + 1, (u + 1) % 2, picks == "sample")
                    if k == 7 and after8 is not None:
                        after8()
                    if k == 13 and picks is not None:
                        gate_exps(n + 1)

            with act.Fori(0, NT - 1) as t:
                x_at = x2_d[bass.ds(t + 1, 1), :, :].rearrange("a p d -> (a p) d")
                h_at = h2_d[bass.ds(t + 1, 1), :, :].rearrange("a p d -> (a p) d")
                q_at = q_dh[bass.ds(t * PH + PH, PH), :, :].rearrange("h p t -> p h t")

                def rms_step():
                    d_rms(reg, t + 1, xd, h2, x_at, P)

                def h2_step():
                    d_store_h2(reg, t + 1, h2, h_at, P)
                    d_keep_h2T(reg, t + 1, mT, 5, P)

                def queries_step():
                    d_store_queries(reg, t + 1, 2, q_at)

                steps = {3: rms_step, 4: h2_step, 5: queries_step}
                for u in range(1, PH + 1):
                    if u == 6:
                        reg(q_stored, t * 16 + 32)
                    act_period(t * PH + u, u, after8=steps.get(u),
                               load=q_dh[bass.ds(t * PH + (u + 2), 1), :, :].rearrange("a p t -> (a p) t"))
                link.restart()

            def sample_rms_step():
                d_rms(reg, NT, xd, h2, x2_d[NT, 0:NS, :], NS)

            def sample_h2_step():
                d_store_h2(reg, NT, h2, h2_d[NT, 0:NS, :], NS)
                d_keep_h2T(reg, NT, mT, 5, NS)

            steps = {3: sample_rms_step, 4: sample_h2_step, 5: d_store_sample_queries}
            for n in range((NT - 1) * PH + 1, NT * PH):
                u = n % PH
                if u == 6:
                    act.wait_ge(q_stored, 16 * (NT + 1))
                act_period(n, n, after8=steps.get(u), load=q_dh[n + 2, :, :], picks="prompt" if n + 1 < NT * PH else "sample")
            act_period(NT * PH, NT * PH, picks="sample")
            act_period(NT * PH + 1, NT * PH + 1, parts=NS, picks=None)
            activate_dots(UNITS - 1, (UNITS - 1) % 2)
            reg(wgt_made, UNITS)
            for k in range(TOPK):
                make_diag(UNITS - 1, (UNITS - 1) % 2, k, NS)

        @block.vector
        def _(dve):
            link = Chain(dve, chain_dve)
            V = nc.vector

            def reg(s, v):
                hold(dve, "dve", s, v)

            dve.wait_ge(exp_c, 1)
            link(V.tensor_scalar(ec9[0:NB + 1, :], ec9[0:NB + 1, :], 1.0, None, ALU.add))
            link(V.reciprocal(ec9[0:NB + 1, :], ec9[0:NB + 1, :]))
            link(V.tensor_tensor(c9[0:NB + 1, :], c9[0:NB + 1, :], ec9[0:NB + 1, :], ALU.mult))
            dve.sem_inc(silu_made, 1)
            dve.wait_ge(small_ps, 1)
            small = banks(6, 1)
            link.note(V.tensor_copy(cT[:, :, :], small[:, 0:72].rearrange("p (k c) -> p k c", k=KC)))
            link.note(V.tensor_copy(state_t[:, :, :], small[:, 72:200].rearrange("p (k c) -> p k c", k=KC)))
            link(V.tensor_copy(cw[:, :, :], small[:, 200:232].rearrange("p (k c) -> p c k", k=KC)))
            dve.sem_inc(small_made, 1)
            dve.sem_inc(ada_free, ARING)
            with dve.Fori(0, NBLK // ARING) as j:
                for r in range(ARING):
                    reg(ada_ps, j * ARING + r + 1)
                    cols = bass.ds(j * (ARING * ABLK) + r * ABLK, ABLK)
                    V.tensor_tensor(mod9[0:NB + 1, cols], banks(r, 1)[0:NB + 1, :], bada9[0:NB + 1, cols],
                                    ALU.add).then_inc(ada_free, 1)
            barrier(dve, 0)

            def first_norm(x, a, b, h, r, rs, parts):
                link(V.reciprocal(rs[0:parts, :], r[0:parts, :]))
                link(V.scalar_tensor_tensor(out=h[0:parts, :], in0=x[0:parts, :], scalar=rs[0:parts, :],
                                            in1=a[0:parts, :], op0=ALU.mult, op1=ALU.mult))
                link(V.tensor_tensor(h[0:parts, :], h[0:parts, :], b[0:parts, :], ALU.add))

            def head_norm(parts):
                link(V.reciprocal(hrs[0:parts, :], hrms[0:parts, :]))
                heads = qkv[0:parts, 0:D + KVW].rearrange("p (h d) -> p h d", h=NQK)
                link(V.tensor_tensor(heads, heads, hrs[0:parts, :].unsqueeze(2).to_broadcast([parts, NQK, HD]), ALU.mult))
                link(V.tensor_tensor(heads, heads, qk_w[0:parts, :, :], ALU.mult))

            dve.wait_ge(rows_in, 16 * 6)
            link(V.scalar_tensor_tensor(out=A1[:, :], in0=A1[:, :], scalar=1.0, in1=junk[:, :], op0=ALU.add, op1=ALU.mult))
            link.note(V.tensor_copy(qk_w[:, 1:NH, :], qk_w[:, 0:1, :].to_broadcast([P, NH - 1, HD])))
            link(V.tensor_copy(qk_w[:, NH + 1:NQK, :], qk_w[:, NH:NH + 1, :].to_broadcast([P, NKV - 1, HD])))
            dve.sem_inc(scale1_made, 1)
            dve.sem_inc(x_free, 2)
            dve.sem_inc(score_read, 1)
            dve.sem_inc(o_kept, 1)
            dve.sem_inc(v_placed, 1)
            dve.sem_inc(hT_kept, 1)
            dve.wait_ge(attn_zeroed, 1)
            link.restart()

            def make_h(wait, n, u):
                wait(rms_made, n + 1)
                first_norm(xt[u], A1, B1, h_row, rms, rstd, P)
                dve.sem_inc(x_free, 1)
                dve.sem_inc(h_made, 1)

            def head_sums(wait, n):
                wait(hss_made, n * 2 + 1)
                link(V.tensor_reduce(hss[:, :], sq[:, :, :], AX.X, ALU.add))
                dve.sem_inc(hss_made, 1)

            def norm_heads(wait, n):
                wait(hrms_made, n + 1)
                head_norm(P)
                dve.sem_inc(qk_normed, 1)

            def place_keys(wait, n, slot):
                wait(qkT_ps, n + 1)
                kT = banks(2, 1)[:, 0:2 * P].rearrange("p (c t) -> p c t", c=2)
                for e in range(2):
                    for half in range(2):
                        link.note(V.tensor_copy(
                            kpad[HD * half:HD * half + HD, :, half, slot, :].rearrange("p (c e) t -> p c e t", e=2)[:, :, e, :],
                            kT[HD * e:HD * e + HD, :, :]))
                link.settle()
                dve.sem_inc(kpad_made, 1)

            def row_max(wait, t, g, u):
                b = g % 2
                wait(score_ps, t * 4 + (g + 1))
                link(V.scalar_tensor_tensor(
                    out=sm[b][:, :, :], in0=banks(3, 2).rearrange("p (h n) -> p h n", h=4), scalar=SCALE,
                    in1=maskt[:, u, :, :].rearrange("p s n -> p (s n)").unsqueeze(1).to_broadcast([P, 4, 2 * P]),
                    op0=ALU.mult, op1=ALU.add))
                dve.sem_inc(score_read, 1)
                link(V.tensor_reduce(smax[:, :], sm[b][:, :, :], AX.X, ALU.max))
                sink_g = sink_row[:, 4 * g:4 * g + 4]
                link(V.tensor_tensor(smax[:, :], smax[:, :], sink_g, ALU.max))
                link.note(V.tensor_scalar(nmax[:, b, :], smax[:, :], -1.0, None, ALU.mult))
                link(V.tensor_tensor(sdif[:, b, :], sink_g, smax[:, :], ALU.subtract))
                dve.sem_inc(max_made, 1)

            def denominators(wait, t, g):
                b = g % 2
                wait(exp_made, t * 4 + (g + 1))
                link(V.tensor_tensor(den[:, b, :], den[:, b, :], esink[:, b, :], ALU.add))
                link(V.reciprocal(rden[:, b, :], den[:, b, :]))
                dve.sem_inc(den_made, 1)

            def copy_pT(wait, t, g):
                wait(pT_ps, t * 4 + (g + 1))
                wait(pv_ps, t * 4 + (g + 4))
                link(V.tensor_copy(pT[:, 1, :, :].rearrange("p h t -> p (h t)"), banks(6, 1)))
                dve.sem_inc(pT1_made, 1)

            def keep_o(wait, t, g):
                wait(pv_ps, t * 4 + (g + 5))
                link(V.tensor_copy(oT[:, 2 * (g - 1):2 * (g - 1) + 4, bass.ds(t * P, P)],
                                   banks(7, 1).rearrange("p (c t) -> p c t", c=4)))
                dve.sem_inc(o_kept, 1)

            def dve_tile(wait, t, u, more, more2):
                row_max(wait, t, 0, u)
                row_max(wait, t, 1, u)
                denominators(wait, t, 0)
                copy_pT(wait, t, 0)
                row_max(wait, t, 2, u)
                denominators(wait, t, 1)
                copy_pT(wait, t, 1)
                row_max(wait, t, 3, u)
                if u == 0:
                    link(V.tensor_copy(maskt[:, 0, :, :], maskt[:, 2, :, :]))
                keep_o(wait, t, 1)
                denominators(wait, t, 2)
                if more:
                    head_sums(wait, t + 1)
                    norm_heads(wait, t + 1)
                copy_pT(wait, t, 2)
                denominators(wait, t, 3)
                if more:
                    place_keys(wait, t + 1, 1 - u)
                copy_pT(wait, t, 3)
                keep_o(wait, t, 3)
                if more2:
                    make_h(wait, t + 2, u)

            w = dve.wait_ge
            make_h(w, 0, 0)
            w(hT_ps, 1)
            make_h(w, 1, 1)
            head_sums(w, 0)
            norm_heads(w, 0)
            place_keys(w, 0, 0)
            link.restart()
            with dve.Fori(0, NT // 2 - 1) as i:
                for u in range(2):
                    dve_tile(reg, i * 2 + u, u, True, True)
                link.restart()
            dve_tile(w, NT - 2, 0, True, False)
            dve_tile(w, NT - 1, 1, False, False)
            barrier(dve, 1)
            dve.wait_ge(s_act, 1)
            dve.wait_ge(srow_in, 48)
            link(V.scalar_tensor_tensor(out=A1[0:NS, :], in0=A1[0:NS, :], scalar=1.0, in1=h_row[0:NS, :], op0=ALU.add, op1=ALU.mult))
            first_norm(xt[0], A1, B1, h_row, rms, rstd, NS)
            dve.sem_inc(s_dve, 1)
            dve.wait_ge(s_kcps, 2)
            for e in range(2):
                for half in range(2):
                    link.note(V.tensor_copy(kcT[HD * half:HD * half + HD, 2 + e, 0:NB * WIN],
                                            banks(5, 2)[HD * e:HD * e + HD, :]))
            link.settle()
            dve.sem_inc(s_kc1, 1)
            dve.wait_ge(s_act, 4)
            link(V.tensor_reduce(hss[0:NS, :], sq[0:NS, :, :], AX.X, ALU.add))
            dve.sem_inc(s_dve, 1)
            dve.wait_ge(s_act, 5)
            head_norm(NS)
            dve.sem_inc(s_dve, 1)
            dve.wait_ge(mask_s_made, 1)
            for q in range(1, 4):
                link.note(V.tensor_copy(s_mask[32 * q:32 * q + 32, :], s_mask[0:NS, :]))
            dve.wait_ge(s_pe, 3)
            qs = banks(0, 1)[:, 0:KC * NS].rearrange("p (g r t) -> p g r t", g=NKV, r=2)
            ks = banks(0, 1)[:, KC * NS:(KC + 2) * NS].rearrange("p (c t) -> p c t", c=2)
            for half in range(2):
                for g in range(NKV):
                    link.note(V.tensor_copy(qz[HD * half:HD * half + HD, g, :, half, :], qs[HD * half:HD * half + HD, g, :, :]))
                for e in range(2):
                    link.note(V.tensor_copy(
                        kcT[HD * half:HD * half + HD, :, NB * WIN:].rearrange("p (c e) t -> p c e t", e=2)[:, :, e, :],
                        ks[HD * e:HD * e + HD, :, :]))
            link.settle()
            dve.wait_ge(s_rows, 64)
            dve.sem_inc(s_dve, 1)
            for g in range(NKV):
                dve.wait_ge(s_pe, 4 + 3 * g)
                link(V.scalar_tensor_tensor(out=s_sm[:, :], in0=banks(3, 3)[:, 0:NB * WIN + NS], scalar=SCALE,
                                            in1=s_mask[:, :], op0=ALU.mult, op1=ALU.add))
                link(V.tensor_reduce(smax[:, 0:1], s_sm[:, :], AX.X, ALU.max))
                link(V.tensor_tensor(smax[:, 0:1], smax[:, 0:1], sink_col[:, g:g + 1], ALU.max))
                link.note(V.tensor_scalar(nmax[:, 0, 0:1], smax[:, 0:1], -1.0, None, ALU.mult))
                link(V.tensor_tensor(sdif[:, 0, 0:1], sink_col[:, g:g + 1], smax[:, 0:1], ALU.subtract))
                dve.sem_inc(s_dve, 1)
                dve.wait_ge(s_act, 6 + 2 * g)
                link(V.tensor_tensor(den[:, 0, 0:1], den[:, 0, 0:1], esink[:, 0, 0:1], ALU.add))
                link(V.reciprocal(rden[:, 0, 0:1], den[:, 0, 0:1]))
                dve.sem_inc(s_dve, 1)
                dve.wait_ge(s_pe, 5 + 3 * g)
                link.note(V.tensor_copy(s_pT[:, 0:NB, :].rearrange("p b t -> p (b t)"), banks(0, 2)))
                link(V.tensor_copy(s_pT[0:NS, NB, :], banks(2, 1)[0:NS, 0:P]))
                dve.sem_inc(s_dve, 1)
                dve.wait_ge(s_pe, 6 + 3 * g)
                e = g % 2
                o_s = banks(6, 1)[HD * e:HD * e + HD, 0:P].rearrange("p (r e t) -> p r e t", r=2, e=2)
                for half in range(2):
                    link.note(V.tensor_copy(oT[HD * half:HD * half + HD, 2 * g:2 * g + 2, NP:T], o_s[:, :, half, :]))
                link.settle()
                dve.sem_inc(s_dve, 1)
            barrier(dve, 2)
            dve.sem_inc(conv_read, 2)
            dve.sem_inc(cu_made, 1)
            link(V.memset(cu_p[:, 0:2], 0.0))
            link.restart()
            for k in range(KC):
                dve.wait_ge(hi_made, k + 1)
                V.tensor_tensor(hT_lo[:, k, :], hT[:, k, :], hT_hi[:, k, :].bitcast(F32), ALU.subtract).then_inc(lo_made, 1)
            dve.sem_inc(w_split, 5)

            def split_lo(i, n):
                reg(w_hi_made, i * 10 + (n + 1))
                reg(conv_ps, i * 10 + (n + 4))
                V.tensor_tensor(w_lo[n % 2][:, :, :], w_c[n % 5][:, :, :], w_hi[n % 2][:, :, :].bitcast(F32), ALU.subtract
                                ).then_inc(w_split, 1)

            def dve_pair(i, last):
                for j in range(2):
                    c = i * 2 + j
                    split_lo(i, 5 * j + 1)
                    b_pre, b_post = (3 * ((5 * j + n) % 2) for n in (1, 2))
                    link.note(V.tensor_copy(cw_now[:, :], cw[:, :, bass.ds(c, 1)].rearrange("p f c -> p (f c)")))
                    link.note(V.tensor_copy(cu_s[:, :, 0:2], state_t[:, bass.ds(c, 1), :].rearrange("p c (b r) -> p (c b) r", b=NB)))
                    split_lo(i, 5 * j + 2)
                    reg(u_made, c + 1)
                    reg(conv_ps, i * 10 + (5 * j + 7))
                    pre = banks(b_pre, 3)
                    link.note(V.tensor_tensor(cu_p[:, 2:], pre[:, 0:NP], u_sb[:, 0:NP], ALU.mult))
                    link(V.tensor_tensor(cu_s[:, :, 2:], pre[:, NP:T].rearrange("p (b l) -> p b l", b=NB),
                                         u_sb[:, NP:T].rearrange("p (b l) -> p b l", b=NB), ALU.mult))
                    dve.sem_inc(conv_read, 1)
                    dve.sem_inc(cu_made, 1)
                    split_lo(i, 5 * j + 3)
                    link.note(V.tensor_copy(new_t[:, bass.ds(c, 1), 0:2].rearrange("p c r -> p (c r)"), cu_p[:, NP:NP + 2]))
                    link.note(V.tensor_copy(new_t[:, bass.ds(c, 1), 2:].rearrange("p c (b r) -> p (c b) r", b=NB),
                                            cu_s[:, :, L:L + 2]))
                    y_p, y_s = y_c[:, 0:NP], y_c[:, NP:T].rearrange("p (b l) -> p b l", b=NB)
                    link.note(V.tensor_scalar(y_p, cu_p[:, 0:NP], cw_now[:, 0:1], cw_now[:, 3:4], ALU.mult, ALU.add))
                    link(V.tensor_scalar(y_s, cu_s[:, :, 0:L], cw_now[:, 0:1], cw_now[:, 3:4], ALU.mult, ALU.add))
                    for tap in (1, 2):
                        link.note(V.scalar_tensor_tensor(out=y_p, in0=cu_p[:, tap:tap + NP], scalar=cw_now[:, tap:tap + 1],
                                                         in1=y_p, op0=ALU.mult, op1=ALU.add))
                        link(V.scalar_tensor_tensor(out=y_s, in0=cu_s[:, :, tap:tap + L], scalar=cw_now[:, tap:tap + 1],
                                                    in1=y_s, op0=ALU.mult, op1=ALU.add))
                    reg(conv_ps, i * 10 + (5 * j + 8))
                    link(V.tensor_tensor(y_c[:, :], banks(b_post, 3)[:, 0:T], y_c[:, :], ALU.mult))
                    dve.sem_inc(conv_read, 1)
                    split_lo(i, 5 * j + 4)
                    reg(gate_c_made, c + 1)
                    if not (last and j == 1):
                        split_lo(i, 5 * j + 5)
                    link(V.tensor_tensor(y_c[:, :], y_c[:, :], sg_c[:, :], ALU.mult))
                    reg(gate_a_made, c + 1)
                    o_c = oT[:, bass.ds(c, 1), :].rearrange("p c t -> p (c t)")
                    link(V.tensor_tensor(mg[:, :], o_c, sg_a[:, :], ALU.mult))
                    link(V.tensor_tensor(o_c, mg[:, :], y_c[:, :], ALU.add))

            split_lo(0, 0)
            with dve.Fori(0, KC // 2 - 1) as i:
                dve_pair(i, False)
                link.restart()
            dve_pair(KC // 2 - 1, True)
            link.restart()
            barrier(dve, 3)
            def d_x2(wait, t, b, x, g, h, parts):
                wait(out_ps, t + 1)
                link(V.tensor_tensor(h[0:parts, :], banks(b, 2)[0:parts, :], g[0:parts, :], ALU.mult))
                link(V.tensor_tensor(x[0:parts, :], x[0:parts, :], h[0:parts, :], ALU.add))
                dve.sem_inc(x2_made, 1)

            def d_h2(wait, t, x, a, b, h, parts):
                wait(rms2_made, t + 1)
                first_norm(x, a, b, h, rms2, rstd2, parts)
                dve.sem_inc(h2_made, 1)

            link(V.tensor_copy(mT[:, :, :], oT[:, :, 0:P]))
            dve.sem_inc(mT_made, 1)
            dve.wait_ge(d_rows, 16 * 4)
            link(V.scalar_tensor_tensor(out=A2[:, :], in0=A2[:, :], scalar=1.0, in1=n2[:, :], op0=ALU.add, op1=ALU.mult))
            dve.wait_ge(xd_in, 16)
            d_x2(dve.wait_ge, 0, 2, xd, G1, h2, P)
            d_h2(dve.wait_ge, 0, xd, A2, B2, h2, P)
            dve.wait_ge(e_consts, 1)
            dve.wait_ge(e_keys_ps, 1)
            kps = banks(0, 2).rearrange("p (h n) -> p h n", h=PH)
            for c in range(2):
                link.note(V.tensor_copy(keys_bd[HD * c:HD * c + HD, 0:PH, PK * c:PK * c + PK], kps[HD * c:HD * c + HD, :, :]))
                link.note(V.tensor_copy(keys_bd[HD * c:HD * c + HD, PH, PK * c:PK * c + PK], kps[HD * c:HD * c + HD, 0, :]))
            link.settle()
            dve.sem_inc(e_keys_made, 1)
            barrier(dve, 4)
            dve.sem_inc(u_free, RING)
            dve.sem_inc(v_free, V_SEED)
            dve.sem_inc(y_read, 1)

            def top16(values, cut, out_v, out_i):
                link(V.max(out_v[:, 0:8], values))
                link.note(V.max_index(out_i[:, 0:8], out_v[:, 0:8], values))
                link(V.match_replace(cut, out_v[:, 0:8], values, LOWEST))
                link(V.max(out_v[:, 8:16], cut))
                link(V.max_index(out_i[:, 8:16], out_v[:, 8:16], cut))

            def pick_half(n, par, c):
                if c == 0:
                    reg(s_out, n + 1)
                top16(s_sb[par][:, c, :], s_cut[:, :], top_v[:, c, :], top_i[:, c, :])

            def pick_best(n):
                link.note(V.tensor_copy(top_f[:, :, :], top_i[:, :, :]))
                link(V.tensor_tensor(cand[:, :, :], top_v[:, 0, :].unsqueeze(2).to_broadcast([P, TOPK, TOPK]),
                                     top_v[:, 1, :].unsqueeze(1).to_broadcast([P, TOPK, TOPK]), ALU.add))
                top16(cand[:, :, :].rearrange("p a b -> p (a b)"), cand_cut[:, :, :].rearrange("p a b -> p (a b)"),
                      best_v[:, :], best_i[:, :])
                link(V.tensor_scalar(nbest[:, :], best_v[:, 0:1], -1.0, None, ALU.mult))
                dve.sem_inc(best_made, 1)

            def pick_key(c):
                op, arg = ((ALU.logical_shift_right, 4), (ALU.bitwise_and, TOPK - 1))[c]
                link(V.tensor_scalar(part_i[:, :], best_i[:, :], arg, None, op))
                link(V.tensor_copy(best_f[:, :], part_i[:, :]))
                link(V.tensor_tensor(onehot[:, :, :], best_f[:, :].unsqueeze(2).to_broadcast([P, TOPK, TOPK]),
                                     iota16[:, :].unsqueeze(1).to_broadcast([P, TOPK, TOPK]), ALU.is_equal))
                link(V.tensor_tensor(onehot[:, :, :], onehot[:, :, :],
                                     top_f[:, c, :].unsqueeze(1).to_broadcast([P, TOPK, TOPK]), ALU.mult))
                link(V.tensor_reduce(i_half[:, c, :], onehot[:, :, :], AX.X, ALU.add))

            def pick_index(buf):
                link(V.scalar_tensor_tensor(out=idx[buf][:, :], in0=i_half[:, 0, :], scalar=float(PK),
                                            in1=i_half[:, 1, :], op0=ALU.mult, op1=ALU.add))
                dve.sem_inc(idx_made, 1)

            def gates(n, par):
                reg(gate_exp, n + 1)
                link(V.reciprocal(gsum[:, :], gsum[:, :]))
                link(V.tensor_scalar(gate[par][:, :], gate_e[:, :], gsum[:, :], None, ALU.mult))

            def weigh(n, par):
                reg(gelu_made, n + 1)
                reg(v_free, n * TOPK + (V_SEED - TOPK))
                link(V.tensor_tensor(wgt[par][:, :], act_dot[par][:, :], gate[par][:, :], ALU.mult))
                dve.sem_inc(wgt_made, 1)

            def dve_period(n, u, weigh_last=True, picks=True, d_step=None):
                par, nxt = u % 2, (u + 1) % 2
                for k in range(TOPK):
                    reg(u_in[k % RING], n * PER_UNIT + 16 * (k // RING + 1))
                    reg(u_free, n * TOPK + (RING + k - 1))
                    V.tensor_tensor_reduce(out=prod[:, k % 2, :], in0=u_ring[k % RING][:, :],
                                           in1=h2_now[:, :], scale=1.0, scalar=0.0, op0=ALU.mult,
                                           op1=ALU.add, accum_out=dot[par][:, k:k + 1]).then_inc(u_free, 1)
                    if k == 0 and weigh_last:
                        weigh(n - 1, nxt)
                    if picks:
                        if k == 1:
                            pick_half(n + 1, nxt, 0)
                        if k == 4:
                            pick_half(n + 1, nxt, 1)
                        if k == 7:
                            pick_best(n + 1)
                        if k == 10:
                            pick_key(0)
                        if k == 12:
                            pick_key(1)
                            pick_index((u + 1) % IDXS)
                if d_step is not None:
                    d_step()
                if picks:
                    gates(n + 1, nxt)

            def take_h2(n, count):
                reg(u_free, n * TOPK + RING)
                reg(h2_in, count)
                link(V.tensor_copy(h2_now[:, :], h2_next[:, :]))
                dve.sem_inc(h2_taken, 1)

            def finish_y(t):
                reg(y_ps, t + 1)
                reg(y_free, t + 1)
                link(V.tensor_tensor(y_now[:, :], banks(0, 2), G2[:, :], ALU.mult))
                dve.sem_inc(y_read, 1)
                reg(x2_in, t * 16 + 16)
                link(V.tensor_tensor(y_now[:, :], y_now[:, :], x2_now[:, :], ALU.add))
                dve.sem_inc(y_made, 1)
                link.restart()

            def d_merged(t):
                reg(qry_ps, t + 1)
                link(V.tensor_copy(mT[:, :, :], oT[:, :, bass.ds(t * P + P, P)]))
                dve.sem_inc(mT_made, 1)

            def d_x2_tile(t, parts):
                reg(xd_in, t * 16 + 32)
                reg(x2h2_stored, t * 32 + 32)
                reg(h2T_ps, t + 1)
                d_x2(reg, t + 1, 2, xd, G1, h2, parts)

            take_h2(0, 16)
            pick_half(0, 0, 0)
            pick_half(0, 0, 1)
            pick_best(0)
            pick_key(0)
            pick_key(1)
            pick_index(0)
            gates(0, 0)
            dve.wait_ge(e_g2_in, 16)
            dve_period(0, 0, weigh_last=False)
            link.restart()
            with dve.Fori(0, NT - 1) as t:
                def merged_step():
                    d_merged(t)

                def x2_step():
                    d_x2_tile(t, P)

                def h2_step():
                    d_h2(reg, t + 1, xd, A2, B2, h2, P)

                steps = {1: merged_step, 2: x2_step, 3: h2_step}
                for u in range(1, PH + 1):
                    if u == PH:
                        take_h2(t * PH + PH, t * 16 + 32)
                    dve_period(t * PH + u, u, d_step=steps.get(u))
                finish_y(t)

            def sample_merged_step():
                dve.wait_ge(qry_ps, NT)
                link(V.tensor_copy(mT[:, :, 0:NS], oT[:, :, NP:T]))
                dve.sem_inc(mT_made, 1)
                dve.wait_ge(d_rows, 16 * 8)
                link(V.scalar_tensor_tensor(out=A2[0:NS, :], in0=A2[0:NS, :], scalar=1.0, in1=n2[0:NS, :],
                                            op0=ALU.add, op1=ALU.mult))

            def sample_x2_step():
                d_x2_tile(NT - 1, NS)

            def sample_h2_step():
                d_h2(reg, NT, xd, A2, B2, h2, NS)

            steps = {1: sample_merged_step, 2: sample_x2_step, 3: sample_h2_step}
            for n in range((NT - 1) * PH + 1, NT * PH):
                dve_period(n, n, d_step=steps.get(n % PH))
            take_h2(NT * PH, 16 * (NT + 4))
            dve_period(NT * PH, NT * PH)
            finish_y(NT - 1)
            dve_period(NT * PH + 1, NT * PH + 1, picks=False)
            weigh(UNITS - 1, (UNITS - 1) % 2)
            dve.wait_ge(y_ps, NT + 1)
            dve.wait_ge(y_free, NT + 1)
            dve.wait_ge(e_g2_in, 32)
            link(V.tensor_tensor(y_now[0:NS, :], banks(0, 2)[0:NS, :], G2[0:NS, :], ALU.mult))
            dve.wait_ge(x2_in, 16 * (NT + 1))
            link(V.tensor_tensor(y_now[0:NS, :], y_now[0:NS, :], x2_now[0:NS, :], ALU.add))
            dve.sem_inc(y_made, 1)

        @block.tensor
        def _(pe):
            M, TR = nc.tensor.matmul, nc.tensor.transpose

            def reg(s, v):
                hold(pe, "pe", s, v)

            pe.wait_ge(consts_made, 1)
            pe.wait_ge(silu_made, 1)
            small = banks(6, 1)
            for rows, n, at in ((c9, NB + 1, 0), (st16, NB * 2, 72), (cw4, 4, 200)):
                for k in range(KC):
                    last = TR(small[:, at + k * n:at + (k + 1) * n], rows[0:n, k * P:(k + 1) * P], ident[0:n, 0:n])
            last.then_inc(small_ps, 1)
            pe.wait_ge(small_made, 1)
            with pe.Fori(0, NBLK // ARING) as j:
                for r in range(ARING):
                    reg(ada_in[r], j * 16 + 16)
                    reg(ada_free, j * ARING + r + 1)
                    for k in range(KC):
                        last = M(banks(r, 1)[0:NB + 1, :], cT[:, k, :], ada_w[r][:, k, :], start=k == 0, stop=k == KC - 1)
                    last.then_inc(ada_ps, 1)
            pe.wait_ge(qkv_w_in, 16)
            barrier(pe, 0)
            pe.wait_ge(attn_zeroed, 1)
            pe.sem_inc(pv_ps, 4)

            def transpose_h(wait, n):
                wait(h_made, n + 1)
                for k in range(KC):
                    last = TR(banks(0, 2)[:, k * P:(k + 1) * P], h_row[:, k * P:(k + 1) * P], ident[:, :])
                last.then_inc(hT_ps, 1)

            def project(c):
                for k in range(KC):
                    last = M(banks(c, 1), hT_now[:, k, :], w_qkv[:, k, c * 512:(c + 1) * 512], start=k == 0, stop=k == KC - 1)
                last.then_inc(qkv_ps, 1)

            def transpose_qk(wait, n):
                wait(qk_normed, n + 1)
                for k in range(KC + 2):
                    last = TR(banks(0, 3)[:, k * P:(k + 1) * P], qkv[:, k * P:(k + 1) * P], ident[:, :])
                last.then_inc(qkT_ps, 1)

            def attend(wait, t, g):
                wait(score_read, t * 4 + (g + 1))
                for pair in range(2):
                    last = M(banks(3 + pair, 1), qT_now[:, 2 * g + pair, :],
                             kpad[:, g, :, :, :].rearrange("p e s n -> p (e s n)"), start=True, stop=True)
                last.then_inc(score_ps, 1)

            def transpose_p(wait, t, g):
                wait(p_made, t * 4 + (g + 1))
                for s in range(2):
                    for h in range(4):
                        last = TR(banks(5 + s, 1)[:, h * P:(h + 1) * P], pe_[g % 2][:, h, s * P:(s + 1) * P], ident[:, :])
                last.then_inc(pT_ps, 1)

            def weigh_values(wait, t, g):
                wait(pT0_made, t * 4 + (g + 1))
                wait(pT1_made, t * 4 + (g + 1))
                if g == 0:
                    wait(v_placed, t + 2)
                if g % 2 == 0:
                    wait(o_kept, t * 2 + (g // 2 + 1))
                for pair in range(2):
                    at = ((g % 2) * 2 + pair) * P
                    for e in range(2):
                        for s in range(2):
                            last = M(banks(7, 1)[:, at:at + P], vpad[:, s, g, HD * e:HD * e + P], pT[:, s, 2 * pair + e, :],
                                     start=e == 0 and s == 0, stop=e == 1 and s == 1)
                last.then_inc(pv_ps, 1)

            def pe_tile(wait, t, more):
                wait(qT_made, t + 1)
                wait(kpad_made, t + 1)
                attend(wait, t, 0)
                if more:
                    transpose_h(wait, t + 1)
                attend(wait, t, 1)
                if more:
                    wait(hT_copied, t + 2)
                    project(0)
                    project(1)
                transpose_p(wait, t, 0)
                attend(wait, t, 2)
                weigh_values(wait, t, 0)
                if more:
                    project(2)
                transpose_p(wait, t, 1)
                attend(wait, t, 3)
                weigh_values(wait, t, 1)
                transpose_p(wait, t, 2)
                weigh_values(wait, t, 2)
                if more:
                    transpose_qk(wait, t + 1)
                transpose_p(wait, t, 3)
                weigh_values(wait, t, 3)

            w = pe.wait_ge
            transpose_h(w, 0)
            w(hT_copied, 1)
            for c in range(3):
                project(c)
            transpose_qk(w, 0)
            with pe.Fori(0, NT // 2 - 1) as i:
                for u in range(2):
                    pe_tile(reg, i * 2 + u, True)
            pe_tile(w, NT - 2, True)
            pe_tile(w, NT - 1, False)
            barrier(pe, 1)
            pe.wait_ge(scache_in, 32)
            for c in range(2):
                for b in range(NB):
                    last = TR(banks(3 + 2 * c, 2)[:, b * P:(b + 1) * P], ck_sb[:, b, c * P:(c + 1) * P], ident[:, :])
                last.then_inc(s_kcps, 1)
            pe.wait_ge(s_dve, 1)
            for k in range(KC):
                last = TR(banks(0, 1)[:, k * NS:(k + 1) * NS], h_row[0:NS, k * P:(k + 1) * P], ident[0:NS, 0:NS])
            last.then_inc(s_pe, 1)
            pe.wait_ge(s_act, 2)
            for c in range(3):
                for k in range(KC):
                    last = M(banks(c, 1)[0:NS, :], hT[:, k, NP:T], w_qkv[:, k, c * 512:(c + 1) * 512], start=k == 0, stop=k == KC - 1)
            last.then_inc(s_pe, 1)
            pe.wait_ge(s_dve, 3)
            for k in range(KC + 2):
                last = TR(banks(0, 1)[:, k * NS:(k + 1) * NS], qkv[0:NS, k * P:(k + 1) * P], ident[0:NS, 0:NS])
            last.then_inc(s_pe, 1)
            pe.wait_ge(s_kc0, 1)
            pe.wait_ge(s_kc1, 1)
            for g in range(NKV):
                pe.wait_ge(s_dve, 4 + 4 * g)
                for at, w in ((0, 512), (512, 512), (1024, NS)):
                    last = M(banks(3, 3)[:, at:at + w], qz[:, g, :, :, :].rearrange("p r e t -> p (r e t)"),
                             kcT[:, g, at:at + w], start=True, stop=True)
                last.then_inc(s_pe, 1)
                pe.wait_ge(s_act, 7 + 2 * g)
                for b in range(NB):
                    TR(banks(0, 2)[:, b * P:(b + 1) * P], s_sm[:, b * P:(b + 1) * P], ident[:, :])
                last = TR(banks(2, 1)[0:NS, 0:P], s_sm[:, NB * P:NB * P + NS], ident[:, :])
                last.then_inc(s_pe, 1)
                pe.wait_ge(s_dve, 7 + 4 * g)
                pair = P * (g // 2)
                for b in range(NB):
                    M(banks(6, 1)[:, 0:P], cv_sb[:, b, pair:pair + P], s_pT[:, b, :], start=b == 0, stop=False)
                last = M(banks(6, 1)[:, 0:P], qkv[0:NS, D + KVW + pair:D + KVW + pair + P], s_pT[0:NS, NB, :], start=False, stop=True)
                last.then_inc(s_pe, 1)
            barrier(pe, 2)
            pe.sem_inc(conv_ps, 5)
            pe.wait_ge(lo_made, KC)
            with pe.Fori(0, KC // 2) as i:
                for n in range(10):
                    reg(w_split, i * 10 + (n + 6))
                    reg(conv_read, i * 10 + (n + 1))
                    b = 3 * (n % 2)
                    for k in range(KC):
                        for w_part, h_part in ((w_hi, hT_hi), (w_hi, hT_lo), (w_lo, hT_hi)):
                            for at, w in ((0, 512), (512, 512), (1024, NS)):
                                last = M(banks(b, 3)[:, at:at + w], w_part[n % 2][:, k, :], h_part[:, k, at:at + w],
                                         start=k == 0 and w_part is w_hi and h_part is hT_hi,
                                         stop=k == KC - 1 and w_part is w_lo)
                    last.then_inc(conv_ps, 1)
            barrier(pe, 3)
            for k in range(KC):
                last = TR(banks(0, 2)[0:2 + NB * 2, k * P:(k + 1) * P], new_t[:, k, :], ident[:, :])
            last.then_inc(new_ps, 1)

            def out_piece(b, m_T, j, parts, of):
                steps = [(c, k) for c in range(2) for k in range(KC)]
                for c, k in steps[j * len(steps) // of:(j + 1) * len(steps) // of]:
                    last = M(banks(b + c, 1)[0:parts, :], m_T[:, k, 0:parts], wo_sb[:, k, c * 512:(c + 1) * 512],
                             start=k == 0, stop=k == KC - 1)
                if j == of - 1:
                    last.then_inc(out_ps, 1)

            def transpose_h2(wait, t, b, h, parts):
                wait(h2_made, t + 1)
                for k in range(KC):
                    last = TR(banks(b, 2)[:, k * P:k * P + parts], h[0:parts, k * P:(k + 1) * P], ident[0:parts, 0:parts])
                last.then_inc(h2T_ps, 1)

            def query_piece(b, h_T, j, parts, of):
                for h in range(j * PH // of, (j + 1) * PH // of):
                    for k in range(KC):
                        last = M(banks(b, 2)[:, h * P:h * P + parts], wq_sb[:, k, h * P:(h + 1) * P], h_T[:, k, 0:parts],
                                 start=k == 0, stop=k == KC - 1)
                if j == of - 1:
                    last.then_inc(qry_ps, 1)

            w = pe.wait_ge
            w(wo_in, 16)
            w(mT_made, 1)
            out_piece(2, mT, 0, P, 1)
            w(new_made, 1)
            w(keys_in, 32)
            for h in range(PH):
                last = TR(banks(0, 2)[:, h * P:(h + 1) * P], keys_row[:, h, :], ident[:, :])
            last.then_inc(e_keys_ps, 1)
            transpose_h2(w, 0, 6, h2, P)
            w(h2T_made, 1)
            w(wq_in, 16)
            query_piece(2, mT, 0, P, 1)
            barrier(pe, 4)

            def scores(n, u, count, sample=False):
                reg(s_out, n)
                reg(q_in[u % 2], count)
                if sample:
                    for q in range(4):
                        last = M(banks(5, 2)[:, 2 * PK * q:2 * PK * q + 2 * PK], q_st[u % 2][:, :],
                                 keys_bd[:, 4 * (n - NT * PH) + q, :], start=True, stop=True)
                    last.then_inc(s_ps, 1)
                else:
                    M(banks(4, 1)[:, 0:2 * PK], q_st[u % 2][:, :], keys_bd[:, u % PH, :], start=True, stop=True).then_inc(s_ps, 1)

            def edge(parts, start, stop):
                for c in range(2):
                    last = M(banks(c, 1)[0:parts, :], zeros_bf[:, 0:parts], zmov_bf[:, :], start=start, stop=stop)
                return last

            pe.wait_ge(q_in[0], 16)
            M(banks(4, 1)[:, 0:2 * PK], q_st[0][:, :], keys_bd[:, 0, :], start=True, stop=True).then_inc(s_ps, 1)
            scores(1, 1, 16)

            def add_rows(n, parts, d_steps={}):
                for k in range(TOPK):
                    if k in d_steps:
                        d_steps[k]()
                    reg(v_in[k % RING], n * PER_UNIT + 16 * (k // RING + 1))
                    reg(diag_made, n * TOPK + (k + 1))
                    for c in range(2):
                        last = M(banks(c, 1)[0:parts, :], diag[k % DIAGS][:, 0:parts], v_ring[k % RING][:, c * 512:(c + 1) * 512],
                                 start=False, stop=False)
                    last.then_inc(v_free, 1)

            def d_steps_of(t, parts):
                def out_step(j):
                    if j == 0:
                        reg(mT_made, t + 2)
                        reg(qry_kept, t + 1)
                    out_piece(2, mT, j, parts, 4)

                def transpose_step():
                    transpose_h2(reg, t + 1, 5, h2, parts)

                def query_step(j):
                    if j == 0:
                        reg(h2T_made, t + 2)
                    query_piece(2, mT, j, parts, 4)

                return {2: {1 + 3 * j: partial(out_step, j) for j in range(4)},
                        4: {0: transpose_step, **{5 + 3 * j: partial(query_step, j) for j in range(4)}}}

            with pe.Fori(0, NT - 1) as t:
                steps = d_steps_of(t, P)
                reg(y_read, t + 1)
                edge(P, True, False)
                for u in range(1, PH + 1):
                    scores(t * PH + (u + 1), u + 1, t * (PH * 8) + 16 * ((u + 1) // 2 + 1))
                    add_rows(t * PH + (u - 1), P, steps.get(u, {}))
                edge(P, False, True).then_inc(y_ps, 1)
            reg(y_read, NT)
            edge(P, True, False)
            steps = d_steps_of(NT - 1, NS)
            for n in range((NT - 1) * PH + 1, NT * PH + 1):
                scores(n + 1, n + 1, 16 * ((n + 1) // 2 + 1), sample=n + 1 >= NT * PH)
                add_rows(n - 1, P, steps.get(n - (NT - 1) * PH, {}))
            edge(P, False, True).then_inc(y_ps, 1)
            reg(y_read, NT + 1)
            edge(NS, True, False)
            for n in range(NT * PH, UNITS):
                add_rows(n, NS)
            edge(NS, False, True).then_inc(y_ps, 1)


_INS = ['x_prompt', 'x_sample', 'cache_k', 'cache_v', 'state_conv', 'c_prompt', 'c_sample',
        'w_ada', 'b_ada', 'norm1_w', 'w_in', 'q_norm_w', 'k_norm_w', 'sinks', 'conv_w', 'conv_bias',
        'w_out', 'norm2_w', 'w_query', 'sub_keys', 'expert_u', 'expert_v']
_OUTS = [(1, NP, D), (NB, L, D), (1, 1, WIN, NKV, HD), (1, 1, WIN, NKV, HD), (1, 1, 2, D),
         (1, NB, WIN, NKV, HD), (1, NB, WIN, NKV, HD), (1, NB, 2, D)]


def kernel(**inputs):
    import numpy as _np
    import concourse.bacc as _bacc
    from concourse import mybir as _mybir
    from concourse.bass_utils import run_bass_kernel_spmd as _run

    nc = _bacc.Bacc("TRN2", target_bir_lowering=False, num_devices=1)
    arrays, args = {}, []
    for name in _INS:
        a = _np.ascontiguousarray(inputs[name])
        arrays[f"in_{name}_dram"] = a
        args.append(nc.dram_tensor(f"in_{name}_dram", a.shape, _mybir.dt.from_np(a.dtype), kind="ExternalInput").ap())
    for i, shape in enumerate(_OUTS):
        args.append(nc.dram_tensor(f"out_{i}_dram", shape, _mybir.dt.float32, kind="ExternalOutput").ap())
    build(nc, *args)
    r = _run(nc, [arrays], core_ids=[0])
    return tuple(r.results[0][f"out_{i}_dram"] for i in range(len(_OUTS)))
```
